# Optimizing a Trainium2 kernel written in Bass

```python
import jax
import jax.numpy as jnp
from jax import lax
import numpy as np

D_MODEL = 1024
BATCH = 1
SEQ = 256
DEPTH = 1
DEC_BATCH = 1
DEC_SEQ = 512
PAST_LEN = 128

RET_HEADS = 8
RET_DK = 64
RET_DV = 64
RET_WIDTH = RET_HEADS * RET_DV
RET_CHUNK = 128
ROPE_BASE = 10000.0
HG_HEADS = 4
HG_DK = 128
HG_DV = 128
HG_KDIM = HG_HEADS * HG_DK
HG_WIDTH = HG_HEADS * HG_DV
HG_CHUNK = 64
HG_SUB = 8
D_FF = 2816
CONV_W = 3
EPS = 1e-6
IN_SPLITS = (RET_HEADS * RET_DK, RET_HEADS * RET_DK, RET_WIDTH, RET_WIDTH,
             HG_KDIM, HG_KDIM, HG_KDIM, HG_WIDTH, HG_WIDTH, D_MODEL, D_MODEL)
D_IN = 2 * RET_HEADS * RET_DK + 2 * RET_WIDTH + 3 * HG_KDIM + 2 * HG_WIDTH + 2 * D_MODEL
F32 = jnp.float32

kernel_name = "hybrid_retention_hgrn2_convffn_encoder"

def rmsnorm(x, w):
    xf = x.astype(F32)
    y = xf * lax.rsqrt(jnp.mean(xf * xf, axis=-1, keepdims=True) + EPS)
    return (y * w.astype(F32)).astype(x.dtype)

def head_rms(o):
    return o * lax.rsqrt(jnp.mean(o * o, axis=-1, keepdims=True) + EPS)

def split_heads(t, n_heads):
    b, l, _ = t.shape
    return t.reshape(b, l, n_heads, -1).transpose(0, 2, 1, 3).astype(F32)

def merge_heads(t):
    b, h, l, d = t.shape
    return t.transpose(0, 2, 1, 3).reshape(b, l, h * d)

def to_chunks(t, c):
    b, h, l, d = t.shape
    return t.reshape(b, h, l // c, c, d)

def flip_seq(t):
    return jnp.flip(t, axis=2)

def rotary(x):
    l, d = x.shape[-2], x.shape[-1]
    half = d // 2
    inv_freq = ROPE_BASE ** (-jnp.arange(half, dtype=F32) / half)
    ang = jnp.arange(l, dtype=F32)[:, None] * inv_freq[None, :]
    cos, sin = jnp.cos(ang), jnp.sin(ang)
    x1, x2 = x[..., :half], x[..., half:]
    return jnp.concatenate([x1 * cos - x2 * sin, x1 * sin + x2 * cos], axis=-1)

def chunk_state_scan(decay, ds):
    def step(s, inp):
        a, d = inp
        return a * s + d, s
    _, prev = lax.scan(step, jnp.zeros(ds.shape[1:], ds.dtype), (decay, ds))
    return prev

def retention_dir(q, k, v, log_gamma, inclusive):
    C = RET_CHUNK
    qc, kc, vc = to_chunks(q, C), to_chunks(k, C), to_chunks(v, C)
    idx = jnp.arange(C, dtype=F32)
    lg = log_gamma[:, None, None]
    diff = idx[:, None] - idx[None, :]
    mask = (diff >= 0) if inclusive else (diff > 0)
    dmat = jnp.where(mask, jnp.exp(jnp.where(mask, diff, 0.0) * lg), 0.0)
    scores = jnp.einsum('bhnid,bhnjd->bhnij', qc, kc) * dmat[None, :, None]
    o_intra = jnp.einsum('bhnij,bhnje->bhnie', scores, vc)
    k_w = kc * jnp.exp((C - 1.0 - idx)[:, None] * lg)[None, :, None]
    ds = jnp.einsum('bhncd,bhnce->bhnde', k_w, vc)
    ds_n = jnp.moveaxis(ds, 2, 0)
    decay = jnp.broadcast_to(jnp.exp(C * log_gamma)[None, None, :, None, None],
                             (ds_n.shape[0], 1, ds_n.shape[2], 1, 1))
    prev = jnp.moveaxis(chunk_state_scan(decay, ds_n), 0, 2)
    q_w = qc * jnp.exp((idx + 1.0)[:, None] * lg)[None, :, None]
    o_cross = jnp.einsum('bhncd,bhnde->bhnce', q_w, prev)
    return (o_intra + o_cross).reshape(v.shape)

def hgrn2_dir(q, k, v, g):
    C, c = HG_CHUNK, HG_SUB
    ns = C // c
    qc, kc, vc, gc = [to_chunks(t, C) for t in (q, k, v, g)]
    b = jnp.cumsum(gc, axis=-2)
    b_last = b[..., -1:, :]
    ds = jnp.einsum('bhncd,bhnce->bhnde', kc * jnp.exp(b_last - b), vc)
    decay = jnp.swapaxes(jnp.moveaxis(jnp.exp(b_last), 2, 0), -1, -2)
    prev = jnp.moveaxis(chunk_state_scan(decay, jnp.moveaxis(ds, 2, 0)), 0, 2)
    o_cross = jnp.einsum('bhncd,bhnde->bhnce', qc * jnp.exp(b), prev)
    sh = qc.shape[:3] + (ns, c, qc.shape[-1])
    qs, ks, bs = qc.reshape(sh), kc.reshape(sh), b.reshape(sh)
    vs = vc.reshape(qc.shape[:3] + (ns, c, vc.shape[-1]))
    b_start = jnp.concatenate([jnp.zeros_like(bs[..., :1, -1:, :]), bs[..., :-1, -1:, :]],
                              axis=-3)
    q_t = qs * jnp.exp(bs - b_start)
    before = jnp.arange(C)[None, :] < (jnp.arange(ns) * c)[:, None]
    rel = b_start - b[..., None, :, :]
    k_t = kc[..., None, :, :] * jnp.where(before[:, :, None], jnp.exp(jnp.minimum(rel, 0.0)), 0.0)
    a_inter = jnp.einsum('bhnaid,bhnajd->bhnaij', q_t, k_t)
    o_inter = jnp.einsum('bhnaij,bhnje->bhnaie', a_inter, vc)
    tri = jnp.arange(c)[:, None] >= jnp.arange(c)[None, :]
    rel_d = bs[..., :, None, :] - bs[..., None, :, :]
    dec = jnp.where(tri[..., None], jnp.exp(jnp.minimum(rel_d, 0.0)), 0.0)
    a_diag = jnp.einsum('bhnaid,bhnajd,bhnaijd->bhnaij', qs, ks, dec)
    o_diag = jnp.einsum('bhnaij,bhnaje->bhnaie', a_diag, vs)
    o_sub = (o_inter + o_diag).reshape(vc.shape)
    return (o_cross + o_sub).reshape(v.shape)

def token_mixer(hn, w_in, lb, w_ret_norm, w_hg_norm, w_ret_up, w_hg_up, w_out):
    dt = hn.dtype
    proj = hn @ w_in
    offsets = np.cumsum(IN_SPLITS)[:-1].tolist()
    rq, rk, rv, rg, hq, hf_fwd, hf_bwd, hi, hg, ga, gb = jnp.split(proj, offsets, axis=-1)

    q = rotary(split_heads(rq, RET_HEADS))
    k = rotary(split_heads(rk, RET_HEADS)) * RET_DK ** -0.5
    v = split_heads(rv, RET_HEADS)
    log_gamma = jnp.log(1.0 - 2.0 ** (-5.0 - jnp.arange(RET_HEADS, dtype=F32)))
    o_ret = (retention_dir(q, k, v, log_gamma, True)
             + flip_seq(retention_dir(flip_seq(q), flip_seq(k), flip_seq(v), log_gamma, False)))
    ret = merge_heads(head_rms(o_ret)) * w_ret_norm.astype(F32) * jax.nn.silu(rg.astype(F32))

    q2 = jax.nn.silu(split_heads(hq, HG_HEADS))
    i2 = split_heads(hi, HG_HEADS)

    def forget(pre, lower):
        f = lower + (1.0 - lower) * jax.nn.sigmoid(pre.astype(F32))
        return split_heads(1.0 - f, HG_HEADS), split_heads(jnp.log(f), HG_HEADS)

    k_f, g_f = forget(hf_fwd, lb[0])
    k_b, g_b = forget(hf_bwd, lb[1])
    o_hg = (hgrn2_dir(q2, k_f, i2, g_f)
            + flip_seq(hgrn2_dir(flip_seq(q2), flip_seq(k_b), flip_seq(i2), flip_seq(g_b))))
    hgo = merge_heads(head_rms(o_hg)) * w_hg_norm.astype(F32) * jax.nn.silu(hg.astype(F32))

    merged = (jax.nn.sigmoid(ga.astype(F32)) * (ret.astype(dt) @ w_ret_up).astype(F32)
              + jax.nn.sigmoid(gb.astype(F32)) * (hgo.astype(dt) @ w_hg_up).astype(F32))
    return merged.astype(dt) @ w_out

def conv_ffn(hn, w_ffn_in, conv_w, conv_b, w_ffn_down):
    dt = hn.dtype
    u, v = jnp.split(hn @ w_ffn_in, 2, axis=-1)
    pad = CONV_W // 2
    up = jnp.pad(u, ((0, 0), (pad, pad), (0, 0)))
    L = u.shape[1]
    uc = conv_b
    for t in range(CONV_W):
        uc = uc + up[:, t:t + L] * conv_w[t]
    return (jax.nn.gelu(uc) * v).astype(dt) @ w_ffn_down

def encode(x, w_in, lower_bounds, w_ret_norm, w_hg_norm, w_ret_up, w_hg_up, w_out,
           norm_mix, norm_ffn, w_ffn_in, conv_w, conv_b, w_ffn_down, norm_final):
    lbs = jnp.cumsum(jax.nn.softmax(lower_bounds.astype(F32), axis=0), axis=0)
    h = x
    for l in range(DEPTH):
        h = h + token_mixer(rmsnorm(h, norm_mix[l]), w_in[l], lbs[l], w_ret_norm[l],
                            w_hg_norm[l], w_ret_up[l], w_hg_up[l], w_out[l])
        h = h + conv_ffn(rmsnorm(h, norm_ffn[l]), w_ffn_in[l], conv_w[l], conv_b[l],
                         w_ffn_down[l])
    return rmsnorm(h, norm_final)

def setup_inputs(seed: int = 0) -> dict:
    key = jax.random.key(seed)
    ks = jax.random.split(key, 16)

    def dense(k, shape, fan_in):
        return jax.random.normal(k, shape, F32) * fan_in ** -0.5

    def gain(k, shape):
        return 1.0 + 0.02 * jax.random.normal(k, shape, F32)

    return {
        "x_prompt": jax.random.normal(ks[0], (BATCH, SEQ, D_MODEL), F32),
        "x_sample": jax.random.normal(ks[1], (DEC_BATCH, DEC_SEQ, D_MODEL), F32),
        "w_in": dense(ks[2], (DEPTH, D_MODEL, D_IN), D_MODEL),
        "lower_bounds": 0.1 * jax.random.normal(ks[3], (DEPTH + 1, 2, HG_KDIM), F32),
        "w_ret_norm": gain(ks[4], (DEPTH, RET_WIDTH)),
        "w_hg_norm": gain(ks[5], (DEPTH, HG_WIDTH)),
        "w_ret_up": dense(ks[6], (DEPTH, RET_WIDTH, D_MODEL), RET_WIDTH),
        "w_hg_up": dense(ks[7], (DEPTH, HG_WIDTH, D_MODEL), HG_WIDTH),
        "w_out": dense(ks[8], (DEPTH, D_MODEL, D_MODEL), D_MODEL),
        "norm_mix": gain(ks[9], (DEPTH, D_MODEL)),
        "norm_ffn": gain(ks[10], (DEPTH, D_MODEL)),
        "w_ffn_in": dense(ks[11], (DEPTH, D_MODEL, 2 * D_FF), D_MODEL),
        "conv_w": dense(ks[12], (DEPTH, CONV_W, D_FF), CONV_W),
        "conv_b": 0.01 * jax.random.normal(ks[13], (DEPTH, D_FF), F32),
        "w_ffn_down": dense(ks[14], (DEPTH, D_FF, D_MODEL), D_FF),
        "norm_final": gain(ks[15], (D_MODEL,)),
    }

def reference(x_prompt, x_sample, w_in, lower_bounds, w_ret_norm, w_hg_norm, w_ret_up,
              w_hg_up, w_out, norm_mix, norm_ffn, w_ffn_in, conv_w, conv_b, w_ffn_down,
              norm_final):
    y_prompt = encode(x_prompt, w_in, lower_bounds, w_ret_norm, w_hg_norm, w_ret_up, w_hg_up,
                      w_out, norm_mix, norm_ffn, w_ffn_in, conv_w, conv_b, w_ffn_down,
                      norm_final)
    y_sample = encode(x_sample, w_in, lower_bounds, w_ret_norm, w_hg_norm, w_ret_up, w_hg_up,
                      w_out, norm_mix, norm_ffn, w_ffn_in, conv_w, conv_b, w_ffn_down,
                      norm_final)
    return (y_prompt, y_sample)


_drawn_inputs = setup_inputs


def setup_inputs(seed=0):
    import zlib

    import numpy as np

    out = dict(_drawn_inputs(seed))
    spreads = {}
    factors = {'lower_bounds': 8.0,
     'w_ret_norm': 28.754,
     'w_hg_norm': 27.09,
     'norm_mix': 3.305,
     'norm_ffn': 14.338,
     'conv_b': 39.736,
     'norm_final': 8.191}
    for name, (base, spread) in spreads.items():
        noise = np.random.default_rng([zlib.crc32(name.encode()), seed]).standard_normal(out[name].shape)
        drawn = base * np.exp(spread * noise) if base else spread * noise
        out[name] = jnp.asarray(drawn.astype(out[name].dtype))
    for name, factor in factors.items():
        out[name] = (out[name] * factor).astype(out[name].dtype)
    return out
```

```python
from contextlib import ExitStack

import numpy as np

import concourse.bass as bass
from concourse import mybir

ALU = mybir.AluOpType
ACT = mybir.ActivationFunctionType
F32 = mybir.dt.float32
F32R = mybir.dt.float32r
U32 = mybir.dt.uint32

P = 128
D = 1024
KD = D // P
NS, NP = 512, 256
T = NS + NP
NT = T // P
GROUPS = ((0, NS), (NS, NP))
HEADS_R, DK_R = 8, 64
PAIRS = HEADS_R // 2
HEADS_H = 4
NH = HEADS_R + HEADS_H
FF = 2816
NF = FF // P
EPS = 1e-6
STRIP = NS + 3 * P
FA = 12
UNIT = 1024

U_MIX = 8
U_HG = U_MIX * HEADS_H
U_UP = U_HG + HEADS_H
U_O0 = U_UP + 3 * KD
U_O1 = U_O0 + 4
U_FA = U_O1 + 4
U_DA = U_FA + 2 * FA
U_FB = U_DA + FA
U_DB = U_FB + 2 * (NF - FA)
UNITS = U_DB + NF - FA

V_MIX, V_FFN, V_GATE, V_CONV, V_LB = 0, 8, 16, 24, 24 + 4 * NF
V_N = V_LB + 16

LEVELS = [1 << i for i in range(9)]
JOBS = ["diag", 1, 2, 4, "hgT", 8, 16, 32, 64, 128, 256, "hgPV", "rvT"]
NJ = len(JOBS)
MERGED = ["diag", 1, 2, 4, 8, 16, 32, 64]
MOVED = ["hgT", 128, 256, "hgPV", "rvT"]


def strided(ap, offset, dims):
    return bass.AP(tensor=ap.tensor, offset=ap.offset + offset, ap=[list(ap.ap[0])] + dims)


def facing(ap, s, t0, n):
    return strided(ap, t0, [[2 * s, n // (2 * s)], [T + s, 2], [1, s]])


def after(eng, sem, value):
    if not isinstance(value, int) or value > 0:
        eng.wait_ge(sem, value)


def at(i):
    return bass.ds(i, 1)


def build(nc, x_s, x_p, units, vec, w_final, ident_d, masks_d, rot_d, strips_d, sel_d, selT_d, y_s, y_p):
    with ExitStack() as ctx:
        def sem(name):
            return ctx.enter_context(nc.semaphore(name))

        def persistent(name, shape, dtype=F32):
            return ctx.enter_context(nc.sbuf_tensor(name, shape, dtype))

        def region(*tensors):
            with ExitStack() as phase:
                return [phase.enter_context(nc.sbuf_tensor(n, s, d)) for n, s, d in tensors]

        raw = persistent("raw", [P, 2, UNIT])
        split = persistent("split", [P, 4, 2, UNIT], F32R)
        hn = persistent("hn", [P, 2, KD, T], F32R)
        ident = persistent("ident", [P, P])
        vecs = persistent("vecs", [P, V_N])
        lb = persistent("lb", [P, 2, 8])
        lbt = persistent("lbt", [P, 3, 8])
        stat = persistent("stat", [P, 4, NT])

        x_in, xn, y32, junk = region(
            ("x_in", [P, NT, D], F32), ("xn0", [P, 2, D], F32), ("y32_0", [P, D], F32), ("junk0", [P, D], F32))
        (oT, gate, rot, masks, sel, selT, tree_t, tree_q, tree_k, qh, yc, pt, vT, hv, swp,
         sig, qT, kT, rv, strips) = region(
            ("oT", [P, KD, T], F32), ("gate", [P, KD, T], F32), ("rot", [P, 2, T], F32),
            ("masks", [P, 7, P], F32), ("sel", [P, KD, NH], F32), ("selT", [NH, KD, P], F32),
            ("tree_t", [P, 4 * T], F32), ("tree_q", [P, 2, T], F32), ("tree_k", [P, 2, T], F32),
            ("qh", [P, T], F32), ("yc", [P, T], F32), ("pt", [P, 4 * NS + 2 * NP], F32),
            ("vT", [P, T], F32), ("hv", [P, T], F32), ("swp", [P, T], F32),
            ("sig", [P, 2, T], F32), ("qT", [P, T], F32), ("kT", [P, T], F32), ("rv", [P, T], F32),
            ("strips", [P, 2, STRIP], F32))
        _, _, rms, _, _, _, gated, _, _, sq, tg = region(
            ("a0", [P, KD, T], F32), ("a1", [P, KD, T], F32), ("rms", [NH, 2, T], F32),
            ("a3", [P, 7, P], F32), ("a4", [P, KD, NH], F32), ("a5", [P, KD * P], F32),
            ("gated", [P, 2, KD, T], F32R), ("a6", [P, 256], F32),
            ("a7", [P, 2, T], F32), ("sq", [P, 2, T], F32), ("tg", [P, 2, T], F32))
        (merged,) = region(("merged", [P, 2, KD, T], F32R))
        _, h, hxn, hy32, hjunk, wfin = region(
            ("b0", [P, 2 * FA * T], F32), ("h", [P, NT, D], F32), ("hxn", [P, 2, D], F32),
            ("hy32", [P, D], F32), ("hjunk", [P, D], F32), ("wfin", [P, D], F32))
        g, _, cb, gl, g32 = region(
            ("g", [P, 2, FA, T], F32R), ("c0", [P, NT * D], F32), ("cb", [P, T], F32),
            ("gl", [P, T], F32), ("g32", [P, T], F32))

        ps = ctx.enter_context(nc.psum_tensor("ps", [P, 8, 512], F32))
        psf = ps[:].rearrange("p b n -> p (b n)")

        x_ld = [sem(f"x_loaded{t}") for t in range(NT)]
        raw_ld = [sem("raw0_loaded"), sem("raw1_loaded")]
        vec_ld, mix_ld, strip_ld, fin_ld, out_st = sem("vec_loaded"), sem("mix_loaded"), sem("strip_loaded"), sem("fin_loaded"), sem("out_stored")
        h_ld = sem("h_loaded")
        hi_split, lo_split, unit_done = sem("hi_split"), sem("lo_split"), sem("unit_done")
        dfree = [sem("dense0_free"), sem("dense1_free")]
        sq_done, var_done, sd_done, xn_done, tr_done, y_done, yhi_done, ylo_done = (
            sem(n) for n in ("sq_done", "var_done", "sd_done", "xn_done", "tr_done", "y_done", "yhi_done", "ylo_done"))
        lb_max, lb_exp, lb_done = sem("lb_max"), sem("lb_exp"), sem("lb_done")
        sg, sc = sem("sigmoid_done"), sem("sigmoid_used")
        vt_done, swap_done, rot_done = sem("vT_done"), sem("swap_done"), sem("rotary_done")
        rs, rp, rpv, ro = sem("ret_scores"), sem("ret_decayed"), sem("ret_pv"), sem("ret_out")
        qk_done, q_up, k_up, yc_done = sem("qk_done"), sem("q_updated"), sem("k_updated"), sem("yc_done")
        mj, mg, mv = sem("mixer_job"), sem("mixer_merged"), sem("mixer_moved")
        sqh, ssum, veps, sdh, rcp, bc, gm, ghi, glo = (
            sem(n) for n in ("head_sq", "head_sum", "head_var", "head_sd", "head_rcp", "head_bcast", "gated32", "gated_hi", "gated_lo"))
        upf, m32, mhi, mlo = sem("up_free"), sem("merged32"), sem("merged_hi"), sem("merged_lo")
        w_done, h_up = sem("wout_done"), sem("h_updated")
        u_free, v_free, c_done, conv_done, gelu_done, g32_done, g_hi, g_lo = (
            sem(n) for n in ("u_free", "v_free", "centre_done", "conv_done", "gelu_done", "g32_done", "g_hi", "g_lo"))
        dn, out_rdy, drv = sem("down_done"), sem("out_ready"), sem("head_var_done")

        blk = ctx.enter_context(nc.Block())

        @blk.sync
        def _(sp):
            def load(n, parity):
                after(sp, lo_split, n - 1)
                src = units[n] if isinstance(n, int) else units[at(n), :, :].rearrange("a p n -> (a p) n")
                sp.dma_start(raw[:, parity, :], src).then_inc(raw_ld[parity], 16)

            xs = x_s.rearrange("(t p) d -> t p d", p=P)
            xp = x_p.rearrange("(t p) d -> t p d", p=P)
            for t in range(NT):
                sp.dma_start(x_in[:, t, :], xs[t] if t < 4 else xp[t - 4]).then_inc(x_ld[t], 16)

            def mixer_loads(hd):
                for u in range(U_MIX):
                    load(hd * U_MIX + u, u % 2)
                    if u == 5:
                        after(sp, rp, 12 * hd)
                        src = strips_d[hd] if isinstance(hd, int) else strips_d[at(hd), :, :].rearrange("a p n -> (a p) n")
                        sp.dma_start(strips[:].rearrange("p a n -> p (a n)"), src).then_inc(strip_ld, 16)

            mixer_loads(0)
            with sp.Fori(1, HEADS_H) as hd:
                mixer_loads(hd)
            with sp.Fori(U_HG // 2, (U_O0 + 4) // 2) as i:
                load(2 * i, 0)
                load(2 * i + 1, 1)
            sp.wait_ge(unit_done, U_O0)
            sp.dma_start(h[:, 0:4, :], x_s.rearrange("(t p) d -> p t d", p=P)).then_inc(h_ld, 16)
            sp.dma_start(h[:, 4:6, :], x_p.rearrange("(t p) d -> p t d", p=P)).then_inc(h_ld, 16)
            sp.wait_ge(sc, 20 + 2 * KD)
            sp.dma_start(wfin[:], w_final).then_inc(fin_ld, 16)
            with sp.Fori((U_O0 + 4) // 2, UNITS // 2) as i:
                load(2 * i, 0)
                load(2 * i + 1, 1)
            ys = y_s.rearrange("(t p) d -> t p d", p=P)
            yp = y_p.rearrange("(t p) d -> t p d", p=P)
            for t in range(NT):
                sp.wait_ge(out_rdy, t + 1)
                sp.dma_start(ys[t] if t < 4 else yp[t - 4], h[:, t, :]).then_inc(out_st, 16)
            sp.wait_ge(out_st, 16 * NT)

        @blk.scalar
        def _(act):
            act.dma_start(vecs[:], vec).then_inc(vec_ld, 16)
            act.dma_start(ident[:], ident_d).then_inc(vec_ld, 16)

            def split_hi(n, slot):
                after(act, raw_ld[slot % 2], 8 * (n - slot % 2) + 16)
                after(act, unit_done, n - 3)
                act.activation(split[:, slot, 0, :], raw[:, slot % 2, :], ACT.Copy).then_inc(hi_split, 1)

            split_hi(0, 0)
            split_hi(1, 1)

            def square(src, t, base, out):
                act.activation(out, src, ACT.Square, accum_out=stat[:, 0, t:t + 1]).then_inc(sq_done, 1)

            def sqrt(t, base):
                act.wait_ge(var_done, base + t + 1)
                act.activation(stat[:, 2, t:t + 1], stat[:, 1, t:t + 1], ACT.Sqrt).then_inc(sd_done, 1)

            def norm_hi(t, base, y):
                act.wait_ge(y_done, base + t + 1)
                act.activation(hn[:, 0, :, t * P:(t + 1) * P], y[:].rearrange("p (k n) -> p k n", k=KD),
                               ACT.Copy).then_inc(yhi_done, 1)

            for t in range(NT + 1):
                if t < NT:
                    act.wait_ge(x_ld[t], 16)
                    square(x_in[:, t, :], t, 0, junk[:])
                    sqrt(t, 0)
                if t > 0:
                    norm_hi(t - 1, 0, y32)
            act.wait_ge(xn_done, NT)
            act.dma_start(rot[:], rot_d).then_inc(mix_ld, 16)
            act.dma_start(masks[:], masks_d).then_inc(mix_ld, 16)
            act.dma_start(sel[:], sel_d).then_inc(mix_ld, 16)
            act.dma_start(selT[:], selT_d).then_inc(mix_ld, 16)
            act.wait_ge(lb_max, 1)
            act.activation(lbt[:, 0:2, :], lb[:], ACT.Exp).then_inc(lb_exp, 1)

            def dense(u):
                return ps[:, 2 * (u % 2):2 * (u % 2) + 2, :].rearrange("p b n -> p (b n)")[:, 0:T]

            def pair(j):
                return ps[:, 4 + 2 * (j % 2):6 + 2 * (j % 2), :].rearrange("p b n -> p (b n)")

            def sigmoid(n, i, u, frees):
                act.wait_ge(unit_done, n + 1)
                after(act, sc, i - 2)
                ins = act.activation(sig[:, u % 2, :], dense(u), ACT.Sigmoid)
                ins.then_inc(sg, 1)
                return ins

            def free_dense(u):
                act.drain().then_inc(dfree[u % 2], 1)

            def copy_y(hd, level):
                i = level.bit_length() - 1
                act.wait_ge(k_up, 9 * hd + 1 + i)
                before = "diag" if i == 0 else LEVELS[i - 1]
                act.wait_ge(mj, NJ * hd + JOBS.index(before) + 1)
                act.activation(strided(yc[:], 0, [[2 * level, T // (2 * level)], [level, 2], [1, level]]),
                               facing(tree_k[:], level, 0, T), ACT.Copy).then_inc(yc_done, 1)

            def swap(hd, u, i):
                act.wait_ge(unit_done, U_MIX * hd + u + 1)
                after(act, rot_done, 2 * hd + i)
                for q in range(4):
                    to = (q ^ 1) * 32
                    ins = act.activation(swp[to:to + 32, :], dense(u)[q * 32:q * 32 + 32, :], ACT.Copy)
                ins.then_inc(swap_done, 1)

            def turn_v(hd, u, job_before):
                act.wait_ge(unit_done, U_MIX * hd + u + 1)
                after(act, mj, job_before)
                act.activation(vT[:], dense(u), ACT.Copy).then_inc(vt_done, 1)
                free_dense(u)

            def move(hd, job):
                j = JOBS.index(job)
                act.wait_ge(mj, NJ * hd + j + 1)
                src = pair(j)
                if job == "hgT":
                    act.activation(hv[:], src[:, 0:T], ACT.Copy).then_inc(mv, 1)
                elif job == "rvT":
                    act.activation(rv[:], src[:, 0:T], ACT.Copy).then_inc(mv, 1)
                elif job == "hgPV":
                    dst = oT[:, HEADS_H + hd, :] if isinstance(hd, int) else oT[:, at(hd + HEADS_H), :]
                    act.activation(dst, src[:, 0:T] if isinstance(hd, int) else src[:, None, 0:T],
                                   ACT.Copy).then_inc(mv, 1)
                elif job == 128:
                    for off, m in ((P, 0), (NS, 1)):
                        act.activation(strided(pt[:], off, [[2 * NS + 2 * P, 2], [1, P]]),
                                       strided(src, m * P, [[2 * P, 2], [1, P]]), ACT.Copy)
                    act.activation(pt[:, 4 * NS + P:4 * NS + 3 * P], src[:, NS:NS + 2 * P], ACT.Copy).then_inc(mv, 1)
                else:
                    act.activation(strided(pt[:], 2 * P, [[NS, 2], [1, 2 * P]]),
                                   strided(src, 0, [[2 * P, 2], [1, 2 * P]]), ACT.Copy)
                    act.activation(strided(pt[:], 2 * NS, [[NS, 2], [1, 2 * P]]),
                                   strided(src, 4 * P, [[2 * P, 2], [1, 2 * P]]), ACT.Copy).then_inc(mv, 1)

            def ret_out(pr):
                act.wait_ge(rpv, 12 * pr + 12)
                src = pair(1)[:, 0:T]
                dst = oT[:, pr, :] if isinstance(pr, int) else oT[:, at(pr), :]
                act.activation(dst, src if isinstance(pr, int) else pair(1)[:, None, 0:T], ACT.Copy).then_inc(ro, 1)

            def mixer(hd, first):
                n = U_MIX * hd
                if not first:
                    sigmoid(n - 1, 4 * hd, 7, False)
                split_hi(n + 2, 2)
                sigmoid(n, 4 * hd + 1, 0, True)
                free_dense(0)
                split_hi(n + 3, 3)
                sigmoid(n + 1, 4 * hd + 2, 1, True)
                free_dense(1)
                if not first:
                    ret_out(hd - 1)
                split_hi(n + 4, 0)
                sigmoid(n + 2, 4 * hd + 3, 2, False)
                split_hi(n + 5, 1)
                copy_y(hd, 1)
                turn_v(hd, 3, NJ * hd)
                copy_y(hd, 2)
                split_hi(n + 6, 2)
                copy_y(hd, 4)
                swap(hd, 4, 0)
                move(hd, "hgT")
                copy_y(hd, 8)
                split_hi(n + 7, 3)
                copy_y(hd, 16)
                swap(hd, 5, 1)
                copy_y(hd, 32)
                split_hi(n + 8, 0)
                copy_y(hd, 64)
                turn_v(hd, 6, NJ * hd + JOBS.index("hgT") + 1)
                split_hi(n + 9, 1)
                after(act, rpv, 12 * hd)
                for job in (128, 256, "hgPV", "rvT"):
                    move(hd, job)

            mixer(0, True)
            with act.Fori(1, HEADS_H) as hd:
                mixer(hd, False)

            sigmoid(U_HG - 1, 16, 7, False)
            split_hi(U_HG + 2, 2)
            sigmoid(U_HG, 17, 0, False)
            split_hi(U_HG + 3, 3)
            sigmoid(U_HG + 1, 18, 1, False)
            ret_out(PAIRS - 1)
            split_hi(U_HG + 4, 0)
            for i in range(KD):
                if i >= 2:
                    act.wait_ge(ssum, i - 1)
                tile = (i + HEADS_H) % KD
                act.activation(sq[:, i % 2, :], oT[:, tile, :], ACT.Square).then_inc(sqh, 1)
            sigmoid(U_HG + 2, 19, 0, False)
            split_hi(U_HG + 5, 1)
            sigmoid(U_HG + 3, 20, 1, False)
            act.wait_ge(veps, 1)
            act.activation(rms[:, 1, :], rms[:, 0, :], ACT.Sqrt).then_inc(sdh, 1)
            for i in range(KD):
                act.wait_ge(gm, i + 1)
                act.activation(gated[:, 0, i, :], tg[:, i % 2, :], ACT.Copy).then_inc(ghi, 1)

            with act.Fori(0, 2) as i2:
                for jj in range(4):
                    n = U_UP + 12 * i2 + 3 * jj
                    j = 4 * i2 + jj
                    split_hi(n + 2, (3 * jj + 2) % 4)
                    sigmoid(n, 20 + 2 * j + 1, 0, True)
                    free_dense(0)
                    split_hi(n + 3, (3 * jj + 3) % 4)
                    sigmoid(n + 1, 20 + 2 * j + 2, 1, True)
                    free_dense(1)
                    split_hi(n + 4, (3 * jj + 4) % 4)
                    act.wait_ge(m32, j + 1)
                    act.activation(merged[:, 0, at(j), :], tg[:, None, 0, :], ACT.Copy).then_inc(mhi, 1)

            for n in range(U_O0, U_O1):
                split_hi(n + 2, (n + 2) % 4)
            split_hi(U_O1 + 2, 2)
            split_hi(U_O1 + 3, 3)
            for t in range(NT + 1):
                if t < NT:
                    act.wait_ge(h_up, NT + t + 1)
                    square(h[:, t, :], t, NT, hjunk[:])
                    sqrt(t, NT)
                if t > 0:
                    norm_hi(t - 1, NT, hy32)
                if t == NT - 1:
                    split_hi(U_FA, 0)
                    split_hi(U_FA + 1, 1)

            def ffn(u0, f0, steps):
                with act.Fori(0, steps) as i:
                    for ff in range(2):
                        n = u0 + 4 * i + 2 * ff
                        f = f0 + 2 * i + ff
                        split_hi(n + 2, (2 * ff + 2) % 4)
                        act.wait_ge(unit_done, n + 1)
                        act.activation(cb[:], psf[:, 6 * 512:6 * 512 + T], ACT.Identity,
                                       bias=vecs[:, bass.ds(V_CONV + 3 * NF + f, 1)],
                                       scale=vecs[:, bass.ds(V_CONV + NF + f, 1)]).then_inc(c_done, 1)
                        split_hi(n + 3, (2 * ff + 3) % 4)
                        act.wait_ge(conv_done, f + 1)
                        act.activation(gl[:], cb[:], ACT.Gelu_apprx_tanh).then_inc(gelu_done, 1)
                        act.wait_ge(g32_done, f + 1)
                        act.activation(g[:, 0, at(2 * i + ff), :], g32[:, None, :], ACT.Copy).then_inc(g_hi, 1)

            ffn(U_FA, 0, FA // 2)
            for n in range(U_DA, U_FB):
                split_hi(n + 2, (n + 2) % 4)
            act.wait_ge(unit_done, U_FB)
            ffn(U_FB, FA, (NF - FA) // 2)
            for n in range(U_DB, UNITS - 2):
                split_hi(n + 2, (n + 2) % 4)
            for t in range(NT):
                act.wait_ge(h_up, 5 * NT + t + 1)
                square(h[:, t, :], t, 2 * NT, hjunk[:])
                sqrt(t, 2 * NT)

        @blk.vector
        def _(dve):
            def split_lo(n, slot):
                after(dve, hi_split, n + 1)
                dve.tensor_tensor(split[:, slot, 1, :], raw[:, slot % 2, :], split[:, slot, 0, :].bitcast(F32),
                                  ALU.subtract).then_inc(lo_split, 1)

            def variance(t, base):
                dve.wait_ge(sq_done, base + t + 1)
                dve.tensor_scalar(stat[:, 1, t:t + 1], stat[:, 0, t:t + 1], 1.0 / D, EPS, ALU.mult,
                                  ALU.add).then_inc(var_done, 1)

            def scale(src, t, base, out):
                dve.wait_ge(sd_done, base + t + 1)
                dve.reciprocal(stat[:, 3, t:t + 1], stat[:, 2, t:t + 1])
                dve.drain()
                if t >= 2:
                    dve.wait_ge(tr_done, base + t - 1)
                dve.tensor_scalar(out[:, t % 2, :], src, stat[:, 3, t:t + 1], None, ALU.mult).then_inc(xn_done, 1)

            def weigh(t, base, col, bank, y):
                dve.wait_ge(tr_done, base + t + 1)
                dve.tensor_tensor(y[:].rearrange("p (k n) -> p k n", k=KD),
                                  ps[:, bank:bank + 2, :].rearrange("p b (k n) -> p (b k) n", n=P),
                                  vecs[:, col:col + KD, None].broadcast_to([P, KD, P]), ALU.mult).then_inc(y_done, 1)
                dve.wait_ge(yhi_done, base + t + 1)
                dve.tensor_tensor(hn[:, 1, :, t * P:(t + 1) * P], y[:].rearrange("p (k n) -> p k n", k=KD),
                                  hn[:, 0, :, t * P:(t + 1) * P].bitcast(F32), ALU.subtract).then_inc(ylo_done, 1)
                dve.drain()

            dve.wait_ge(vec_ld, 32)
            for t in range(NT + 1):
                if t < NT:
                    variance(t, 0)
                    scale(x_in[:, t, :], t, 0, xn)
                if t > 0:
                    weigh(t - 1, 0, V_MIX, 4 + 2 * ((t - 1) % 2), y32)
                if t == 0:
                    split_lo(0, 0)
                    split_lo(1, 1)
            lrow = vecs[:, V_LB:V_LB + 16].rearrange("p (r c) -> p r c", r=2)
            dve.tensor_tensor(lbt[:, 2, :], lrow[:, 0, :], lrow[:, 1, :], ALU.max)
            dve.drain()
            dve.tensor_tensor(lb[:], lrow, lbt[:, 2:3, :].broadcast_to([P, 2, 8]), ALU.subtract).then_inc(lb_max, 1)
            dve.wait_ge(lb_exp, 1)
            dve.tensor_tensor(lbt[:, 2, :], lbt[:, 0, :], lbt[:, 1, :], ALU.add)
            dve.drain()
            dve.reciprocal(lbt[:, 1, :], lbt[:, 2, :])
            dve.drain()
            dve.tensor_tensor(lb[:, 0, :], lbt[:, 0, :], lbt[:, 1, :], ALU.mult)
            dve.drain()
            dve.tensor_scalar(lb[:, 1, :], lb[:, 0, :], -1.0, 1.0, ALU.mult, ALU.add)
            dve.drain()
            dve.wait_ge(mix_ld, 64)

            def dense(u):
                return ps[:, 2 * (u % 2):2 * (u % 2) + 2, :].rearrange("p b n -> p (b n)")[:, 0:T]

            def pair(j):
                return ps[:, 4 + 2 * (j % 2):6 + 2 * (j % 2), :].rearrange("p b n -> p (b n)")

            def decay(pr, i):
                a, m = divmod(i, 6)
                dve.wait_ge(rs, 12 * pr + i + 1)
                if i >= 4:
                    dve.wait_ge(rpv, 12 * pr + i - 3)
                width = NS if m < 4 else NP
                c0 = STRIP - NS - P * (m % 4)
                dve.tensor_tensor(pt[:, (i % 4) * NS:(i % 4) * NS + width], ps[:, 4 + i % 2, 0:width],
                                  strips[:, a, c0:c0 + width], ALU.mult).then_inc(rp, 1)

            def silu_gate(tile, n, i, u):
                dve.wait_ge(sg, i)
                dst = gate[:, tile, :] if isinstance(tile, int) else gate[:, at(tile), :]
                a, b = (dense(u), sig[:, u % 2, :]) if isinstance(tile, int) else (
                    strided(dense(u), 0, [[T, 1], [1, T]]), sig[:, u % 2:u % 2 + 1, :])
                dve.tensor_tensor(dst, a, b, ALU.mult).then_inc(sc, 1)
                dve.drain().then_inc(dfree[u % 2], 1)

            def forget(hd, d):
                c = 4 * d + hd
                cols = (lb[:, 1, c:c + 1], lb[:, 0, c:c + 1]) if isinstance(c, int) else (lb[:, 1, at(c)], lb[:, 0, at(c)])
                dve.wait_ge(sg, 4 * hd + 1 + d)
                f = tree_t[:, (1 - d) * T:(2 - d) * T]
                dve.tensor_scalar(f, sig[:, d, :], cols[0], cols[1], ALU.mult, ALU.add).then_inc(sc, 1)
                dve.drain()
                dve.tensor_scalar(tree_k[:, d, :], f, -1.0, 1.0, ALU.mult, ALU.add).then_inc(k_up, d)if d else \
                    dve.tensor_scalar(tree_k[:, d, :], f, -1.0, 1.0, ALU.mult, ALU.add)

            def queries(hd):
                dve.wait_ge(sg, 4 * hd + 3)
                dve.tensor_tensor(qh[:], dense(2), sig[:, 0, :], ALU.mult).then_inc(sc, 1)
                dve.drain().then_inc(dfree[0], 1)
                dve.tensor_tensor(tree_q[:], qh[:, None, :].broadcast_to([P, 2, T]),
                                  tree_t[:, 0:2 * T].rearrange("p (a n) -> p a n", a=2), ALU.mult).then_inc(q_up, 1)
                dve.tensor_tensor(yc[:], tree_k[:, 0, :], tree_k[:, 1, :], ALU.add).then_inc(qk_done, 1)

            def totals(s):
                return 0 if s == 1 else 4 * T - 4 * T // s

            def update(hd, s):
                i = s.bit_length() - 1
                n = T if s < 128 else NS
                c, nb = totals(s), T // s
                if s < 128:
                    dve.wait_ge(yc_done, 7 * hd + i + 1)
                else:
                    dve.wait_ge(mj, NJ * hd + JOBS.index(s) + 1)
                keys = facing(tree_k[:], s, 0, n)
                dve.tensor_tensor(keys, keys, strided(tree_t[:], c + nb + 1, [[2, n // (2 * s)], [-(nb + 1), 2], [0, s]]),
                                  ALU.mult).then_inc(k_up, 1)
                if s < 128:
                    dve.wait_ge(mj, NJ * hd + JOBS.index(s) + 1)
                qs = facing(tree_q[:], s, 0, n)
                dve.tensor_tensor(qs, qs, strided(tree_t[:], c + 1, [[2, n // (2 * s)], [nb - 1, 2], [0, s]]),
                                  ALU.mult).then_inc(q_up, 1)
                if s < 128:
                    two = strided(tree_t[:], c, [[nb, 2], [2, nb // 2], [1, 2]])
                    dve.tensor_tensor(strided(tree_t[:], totals(2 * s), [[nb // 2, 2], [1, nb // 2]]),
                                      two[:, :, :, 0], two[:, :, :, 1], ALU.mult)
                    dve.drain()

            def merge(hd, job):
                k, j = MERGED.index(job), JOBS.index(job)
                if job == "diag":
                    dve.wait_ge(mj, NJ * hd + j + 1)
                for off, step, c0, nc_ in ((0, NS + P, 0, 4), (4 * NS, NP + P, 4, 2)):
                    dst = strided(pt[:], off, [[step, nc_], [1, P]])
                    src = strided(pair(j), c0 * P, [[P, nc_], [1, P]])
                    if job == "diag":
                        ins = dve.tensor_tensor(dst, src, ident[:, None, :].broadcast_to([P, nc_, P]), ALU.mult)
                    else:
                        ins = dve.copy_predicated(dst, masks[:, k - 1:k, :].bitcast(U32).broadcast_to([P, nc_, P]), src)
                ins.then_inc(mg, 1)
                dve.drain()

            def rotary(hd, u, i, dst):
                dve.wait_ge(swap_done, 2 * hd + i + 1)
                dve.tensor_tensor(dst[:], dense(u), rot[:, 0, :], ALU.mult)
                dve.tensor_tensor(swp[:], swp[:], rot[:, 1, :], ALU.mult)
                dve.drain().then_inc(dfree[u % 2], 1)
                dve.tensor_tensor(dst[:], dst[:], swp[:], ALU.add).then_inc(rot_done, 1)

            def mixer(hd, first):
                n = U_MIX * hd
                if not first:
                    silu_gate(hd - 1, n - 1, 4 * hd, 7)
                split_lo(n + 2, 2)
                if not first:
                    dve.wait_ge(strip_ld, 16 * hd)
                    dve.wait_ge(mj, NJ * hd)
                    for i in range(6):
                        decay(hd - 1, i)
                forget(hd, 0)
                split_lo(n + 3, 3)
                if not first:
                    for i in range(6, 12):
                        decay(hd - 1, i)
                forget(hd, 1)
                split_lo(n + 4, 0)
                queries(hd)
                split_lo(n + 5, 1)
                after(dve, rpv, 12 * hd)
                merge(hd, "diag")
                update(hd, 1)
                merge(hd, 1)
                split_lo(n + 6, 2)
                update(hd, 2)
                merge(hd, 2)
                update(hd, 4)
                merge(hd, 4)
                after(dve, rs, 12 * hd)
                rotary(hd, 4, 0, qT)
                split_lo(n + 7, 3)
                update(hd, 8)
                merge(hd, 8)
                update(hd, 16)
                merge(hd, 16)
                rotary(hd, 5, 1, kT)
                split_lo(n + 8, 0)
                update(hd, 32)
                merge(hd, 32)
                update(hd, 64)
                merge(hd, 64)
                split_lo(n + 9, 1)
                update(hd, 128)

            mixer(0, True)
            with dve.Fori(1, HEADS_H) as hd:
                mixer(hd, False)

            silu_gate(HEADS_H - 1, U_HG - 1, 16, 7)
            split_lo(U_HG + 2, 2)
            dve.wait_ge(strip_ld, 16 * PAIRS)
            dve.wait_ge(mj, NJ * HEADS_H)
            for i in range(6):
                decay(PAIRS - 1, i)
            silu_gate(HEADS_H, U_HG, 17, 0)
            split_lo(U_HG + 3, 3)
            for i in range(6, 12):
                decay(PAIRS - 1, i)
            silu_gate(HEADS_H + 1, U_HG + 1, 18, 1)
            split_lo(U_HG + 4, 0)
            silu_gate(HEADS_H + 2, U_HG + 2, 19, 0)
            split_lo(U_HG + 5, 1)
            dve.wait_ge(ssum, KD)
            dve.tensor_scalar(rms[:, 0, :], pair(0)[0:NH, 0:T], EPS, None, ALU.add).then_inc(veps, 1)
            silu_gate(HEADS_H + 3, U_HG + 3, 20, 1)
            dve.wait_ge(sdh, 1)
            dve.reciprocal(rms[:, 0, :], rms[:, 1, :]).then_inc(rcp, 1)
            for i in range(KD):
                dve.wait_ge(bc, i + 1)
                if i >= 2:
                    dve.wait_ge(ghi, i - 1)
                dve.scalar_tensor_tensor(out=tg[:, i % 2, :], in0=oT[:, i, :], scalar=vecs[:, V_GATE + i:V_GATE + i + 1],
                                         in1=pair(i + 1)[:, 0:T], op0=ALU.mult, op1=ALU.mult)
                dve.drain().then_inc(drv, 1)
                dve.tensor_tensor(tg[:, i % 2, :], tg[:, i % 2, :], gate[:, i, :], ALU.mult).then_inc(gm, 1)
                if i > 0:
                    dve.wait_ge(ghi, i)
                    dve.tensor_tensor(gated[:, 1, i - 1, :], tg[:, (i - 1) % 2, :], gated[:, 0, i - 1, :].bitcast(F32),
                                      ALU.subtract).then_inc(glo, 1)
                    dve.drain()
            dve.wait_ge(ghi, KD)
            dve.tensor_tensor(gated[:, 1, KD - 1, :], tg[:, 1, :], gated[:, 0, KD - 1, :].bitcast(F32),
                              ALU.subtract).then_inc(glo, 1)
            dve.drain().then_inc(upf, 1)

            with dve.Fori(0, 2) as i2:
                for jj in range(4):
                    n = U_UP + 12 * i2 + 3 * jj
                    j = 4 * i2 + jj
                    split_lo(n + 2, (3 * jj + 2) % 4)
                    split_lo(n + 3, (3 * jj + 3) % 4)
                    split_lo(n + 4, (3 * jj + 4) % 4)
                    dve.wait_ge(sg, 20 + 2 * j + 2)
                    dve.wait_ge(unit_done, n + 3)
                    dve.tensor_tensor(tg[:, 0, :], psf[:, 4 * 512:4 * 512 + T], sig[:, 0, :], ALU.mult).then_inc(sc, 1)
                    dve.tensor_tensor(tg[:, 1, :], psf[:, 6 * 512:6 * 512 + T], sig[:, 1, :], ALU.mult).then_inc(sc, 1)
                    dve.drain().then_inc(upf, 1)
                    dve.tensor_tensor(tg[:, 0, :], tg[:, 0, :], tg[:, 1, :], ALU.add).then_inc(m32, 1)
                    dve.wait_ge(mhi, j + 1)
                    dve.tensor_tensor(merged[:, 1, at(j), :], tg[:, None, 0, :], merged[:, 0, at(j), :].bitcast(F32),
                                      ALU.subtract).then_inc(mlo, 1)
                    dve.drain()

            def residual(t, half, bank):
                hs = h[:, t, 512 * half:512 * half + 512]
                return dve.tensor_tensor(hs, ps[:, bank, :], hs, ALU.add).then_inc(h_up, 1)

            for n in range(U_O0, U_O1):
                split_lo(n + 2, (n + 2) % 4)
            split_lo(U_O1 + 2, 2)
            dve.wait_ge(h_ld, 32)
            for t in range(NT):
                dve.wait_ge(w_done, t + 1)
                residual(t, 0, t)
            split_lo(U_O1 + 3, 3)
            for t in range(NT + 1):
                if t < NT:
                    dve.wait_ge(w_done, NT + t + 1)
                    residual(t, 1, (6 + t) % 8)
                    if t == 1:
                        dve.drain().then_inc(u_free, 1)
                    if t == 3:
                        dve.drain().then_inc(v_free, 1)
                    variance(t, NT)
                    scale(h[:, t, :], t, NT, hxn)
                if t > 0:
                    weigh(t - 1, NT, V_FFN, 4, hy32)
                if t == NT - 1:
                    split_lo(U_FA, 0)
                    split_lo(U_FA + 1, 1)

            def ffn(u0, f0, steps):
                with dve.Fori(0, steps) as i:
                    for ff in range(2):
                        n = u0 + 4 * i + 2 * ff
                        f = f0 + 2 * i + ff
                        split_lo(n + 2, (2 * ff + 2) % 4)
                        dve.wait_ge(c_done, f + 1)
                        for tap, to, frm in ((0, 1, 0), (2, 0, 1)):
                            for c0, w in GROUPS:
                                cs = cb[:, c0 + to:c0 + to + w - 1]
                                dve.scalar_tensor_tensor(
                                    out=cs, in0=psf[:, 6 * 512 + c0 + frm:6 * 512 + c0 + frm + w - 1],
                                    scalar=vecs[:, bass.ds(V_CONV + tap * NF + f, 1)], in1=cs,
                                    op0=ALU.mult, op1=ALU.add)
                            if tap == 0:
                                dve.drain()
                        dve.drain().then_inc(u_free, 1)
                        dve.drain().then_inc(conv_done, 1)
                        split_lo(n + 3, (2 * ff + 3) % 4)
                        dve.wait_ge(gelu_done, f + 1)
                        dve.wait_ge(unit_done, n + 2)
                        dve.tensor_tensor(g32[:], psf[:, 0:T], gl[:], ALU.mult).then_inc(g32_done, 1)
                        dve.drain().then_inc(v_free, 1)
                        dve.wait_ge(g_hi, f + 1)
                        dve.tensor_tensor(g[:, 1, at(2 * i + ff), :], g32[:, None, :],
                                          g[:, 0, at(2 * i + ff), :].bitcast(F32), ALU.subtract).then_inc(g_lo, 1)

            def down(u0, u1, base):
                mid = (u0 + u1) // 2
                for n in range(u0, u1):
                    if n == mid + 1:
                        for t in range(NT):
                            dve.wait_ge(dn, base + t + 1)
                            residual(t, 0, 2 + t)
                    if n + 2 < UNITS:
                        split_lo(n + 2, (n + 2) % 4)

            ffn(U_FA, 0, FA // 2)
            down(U_DA, U_FB, 0)
            for t in range(NT):
                dve.wait_ge(dn, NT + t + 1)
                residual(t, 1, t)
            ffn(U_FB, FA, (NF - FA) // 2)
            down(U_DB, UNITS, 2 * NT)
            dve.wait_ge(fin_ld, 16)
            for t in range(NT):
                dve.wait_ge(dn, 3 * NT + t + 1)
                residual(t, 1, t)
                variance(t, 2 * NT)
                dve.wait_ge(sd_done, 2 * NT + t + 1)
                dve.reciprocal(stat[:, 3, t:t + 1], stat[:, 2, t:t + 1])
                dve.drain()
                dve.scalar_tensor_tensor(out=h[:, t, :], in0=h[:, t, :], scalar=stat[:, 3, t:t + 1], in1=wfin[:],
                                         op0=ALU.mult, op1=ALU.mult).then_inc(out_rdy, 1)

        @blk.tensor
        def _(pe):
            def transposes(src, bank, t, base):
                pe.wait_ge(xn_done, base + t + 1)
                for k in range(KD):
                    ins = pe.transpose(ps[:, bank + k // 4, (k % 4) * P:(k % 4 + 1) * P],
                                       src[:, t % 2, k * P:(k + 1) * P], ident[:])
                ins.then_inc(tr_done, 1)

            pe.wait_ge(vec_ld, 32)
            for t in range(NT):
                if t >= 2:
                    pe.wait_ge(y_done, t - 1)
                transposes(xn, 4 + 2 * (t % 2), t, 0)

            def passes(out, w_slot, w0, w1, m, mt, cols, start, stop, stationary_w=True):
                for i, (a, b) in enumerate(((0, 0), (0, 1), (1, 0))):
                    w = split[:, w_slot, a, w0:w1]
                    x = m[:, b, mt, cols[0]:cols[1]]
                    ins = pe.matmul(out, w if stationary_w else x, x if stationary_w else w,
                                    start=start and i == 0, stop=stop and i == 2)
                return ins

            def part(n, slot, bank, i):
                if i == 0:
                    pe.wait_ge(lo_split, n + 1)
                (c0, w), ks = (GROUPS[0], range(2 * i, 2 * i + 2)) if i < 4 else (GROUPS[1], range(4 * (i - 4), 4 * (i - 4) + 4))
                for k in ks:
                    ins = passes(ps[:, bank + (i >= 4), 0:w], slot, k * P, (k + 1) * P, hn, k, (c0, c0 + w), k == 0, k == KD - 1)
                if i == 5:
                    ins.then_inc(unit_done, 1)

            def banks(j):
                return 4 + 2 * (j % 2)

            def score(pr, i):
                a, m = divmod(i, 6)
                c0, w = GROUPS[m // 4]
                if i >= 2:
                    pe.wait_ge(rp, 12 * pr + i - 1)
                pe.matmul(ps[:, 4 + i % 2, 0:w], kT[64 * a:64 * a + 64, m * P:(m + 1) * P],
                          qT[64 * a:64 * a + 64, c0:c0 + w], start=True, stop=True).then_inc(rs, 1)

            def values(pr, i):
                a, m = divmod(i, 6)
                c0, w = GROUPS[m // 4]
                pe.wait_ge(rp, 12 * pr + i + 1)
                pe.matmul(ps[64 * a:64 * a + 64, 6 + m // 4, 0:w], rv[:, m * P + 64 * a:m * P + 64 * a + 64],
                          pt[:, (i % 4) * NS:(i % 4) * NS + w], start=m in (0, 4), stop=m in (3, 5)).then_inc(rpv, 1)

            def retention_start(pr):
                pe.wait_ge(rot_done, 2 * pr + 2)
                pe.wait_ge(mv, len(MOVED) * (pr + 1))
                score(pr, 0)
                score(pr, 1)

            def retention_part(pr, i):
                values(pr, i)
                if i + 2 < 12:
                    score(pr, i + 2)

            def job(hd, what, first=False):
                j = JOBS.index(what)
                b = banks(j)
                if j == 0:
                    after(pe, rp, 12 * hd)
                    if first:
                        pe.wait_ge(y_done, NT)
                elif j == 1:
                    after(pe, ro, hd)
                elif JOBS[j - 2] in MERGED:
                    pe.wait_ge(mg, len(MERGED) * hd + MERGED.index(JOBS[j - 2]) + 1)
                else:
                    pe.wait_ge(mv, len(MOVED) * hd + MOVED.index(JOBS[j - 2]) + 1)
                out = lambda c0, w: psf[:, b * 512 + c0:b * 512 + c0 + w]
                tok = lambda c: (c * P, (c + 1) * P)
                if what == "diag":
                    pe.wait_ge(qk_done, hd + 1)
                    for c in range(NT):
                        ins = pe.matmul(out(c * P, P), yc[:, c * P:(c + 1) * P], qh[:, c * P:(c + 1) * P], start=True, stop=True)
                elif what in ("hgT", "rvT"):
                    pe.wait_ge(vt_done, 2 * hd + (1 if what == "hgT" else 2))
                    for c in range(NT):
                        ins = pe.transpose(out(c * P, P), vT[:, c * P:(c + 1) * P], ident[:])
                elif what == "hgPV":
                    pe.wait_ge(mg, len(MERGED) * (hd + 1))
                    pe.wait_ge(mv, len(MOVED) * hd + 3)
                    for m in range(NT):
                        c0, w = GROUPS[m // 4]
                        s0 = m * NS if m < 4 else 4 * NS + (m - 4) * NP
                        ins = pe.matmul(out(c0, w), hv[:, m * P:(m + 1) * P], pt[:, s0:s0 + w],
                                        start=m in (0, 4), stop=m in (3, 5))
                elif what < 128:
                    i = what.bit_length() - 1
                    pe.wait_ge(yc_done, 7 * hd + i + 1)
                    pe.wait_ge(q_up, 9 * hd + 1 + i)
                    for c in range(NT):
                        ins = pe.matmul(out(c * P, P), yc[:, c * P:(c + 1) * P], facing(tree_q[:], what, c * P, P),
                                        start=True, stop=True)
                else:
                    i = what.bit_length() - 1
                    pe.wait_ge(q_up, 9 * hd + 1 + i)
                    pe.wait_ge(k_up, 9 * hd + 1 + i)
                    cb_ = what // P
                    for m in range(NT if what == 128 else 4):
                        right = (m // cb_) % 2
                        q0 = (m // (2 * cb_)) * 2 * what + (0 if right else what)
                        ins = pe.matmul(out(m * what, what), tree_k[:, right, m * P:(m + 1) * P],
                                        tree_q[:, 1 - right, q0:q0 + what], start=True, stop=True)
                ins.then_inc(mj, 1)

            WHEN = {(3, 4): "diag", (4, 0): 1, (4, 2): 2, (4, 4): 4, (5, 0): "hgT", (5, 2): 8, (5, 4): 16,
                    (6, 0): 32, (6, 2): 64, (6, 4): 128, (7, 0): 256, (7, 3): "hgPV", (7, 5): "rvT"}

            def mixer(hd, first):
                if not first:
                    retention_start(hd - 1)
                for u in range(U_MIX):
                    after(pe, dfree[u % 2], 4 * hd + u // 2)
                    for i in range(6):
                        part(U_MIX * hd + u, u % 4, 2 * (u % 2), i)
                        if u < 2 and not first:
                            retention_part(hd - 1, 6 * u + i)
                        if (u, i) in WHEN:
                            job(hd, WHEN[u, i], first)

            pe.wait_ge(ylo_done, NT)
            mixer(0, True)
            with pe.Fori(1, HEADS_H) as hd:
                mixer(hd, False)

            retention_start(PAIRS - 1)
            pe.wait_ge(mix_ld, 64)
            for u in range(HEADS_H):
                pe.wait_ge(dfree[u % 2], 16 + u // 2)
                for i in range(6):
                    part(U_HG + u, u, 2 * (u % 2), i)
                    if u < 2:
                        retention_part(PAIRS - 1, 6 * u + i)
                if u == 2:
                    for i in range(KD):
                        pe.wait_ge(sqh, i + 1)
                        tile = (i + HEADS_H) % KD
                        for b, (c0, w) in enumerate(GROUPS):
                            ins = pe.matmul(ps[0:NH, 4 + b, 0:w], sel[:, tile, :], sq[:, i % 2, c0:c0 + w],
                                            start=i == 0, stop=i == KD - 1)
                        ins.then_inc(ssum, 1)
            pe.wait_ge(ro, PAIRS)
            pe.wait_ge(rcp, 1)
            for i in range(KD):
                if i >= 2:
                    pe.wait_ge(drv, i - 1)
                for b, (c0, w) in enumerate(GROUPS):
                    ins = pe.matmul(ps[:, banks(i + 1) + b, 0:w], selT[:, i, :], rms[:, 0, c0:c0 + w],
                                    start=True, stop=True)
                ins.then_inc(bc, 1)

            pe.wait_ge(glo, KD)
            with pe.Fori(0, 2) as i2:
                for jj in range(4):
                    n = U_UP + 12 * i2 + 3 * jj
                    j = 4 * i2 + jj
                    for u in range(2):
                        pe.wait_ge(dfree[u], 18 + j)
                        for i in range(6):
                            part(n + u, (3 * jj + u) % 4, 2 * u, i)
                    pe.wait_ge(lo_split, n + 3)
                    pe.wait_ge(upf, j + 1)
                    for kind in range(2):
                        for b, (c0, w) in enumerate(GROUPS):
                            for k in range(4 * kind, 4 * kind + 4):
                                ins = passes(ps[:, 4 + 2 * kind + b, 0:w], (3 * jj + 2) % 4, k * P, (k + 1) * P,
                                             gated, k, (c0, c0 + w), k % 4 == 0, k % 4 == 3)
                    ins.then_inc(unit_done, 1)

            def rows(n, k2, m, mt, t, bank, start, stop):
                return passes(ps[:, bank, :], n % 4, 512 * k2, 512 * k2 + 512, m, mt, (t * P, (t + 1) * P),
                              start, stop, stationary_w=False)

            pe.wait_ge(dfree[0], 26)
            pe.wait_ge(dfree[1], 26)
            pe.wait_ge(upf, KD + 1)
            for k in range(KD):
                n = U_O0 + k // 2
                if k % 2 == 0:
                    pe.wait_ge(lo_split, n + 1)
                pe.wait_ge(mlo, k + 1)
                for t in range(NT):
                    ins = rows(n, k % 2, merged, k, t, t, k == 0, k == KD - 1)
                    if k == KD - 1:
                        ins.then_inc(w_done, 1)
                if k % 2 == 1:
                    pe.drain().then_inc(unit_done, 1)
            for t in range(NT + 1):
                if t < NT:
                    if t >= 2:
                        pe.wait_ge(h_up, t - 1)
                    for k in range(KD):
                        n = U_O1 + k // 2
                        if t == 0 and k % 2 == 0:
                            pe.wait_ge(lo_split, n + 1)
                        ins = rows(n, k % 2, merged, k, t, (6 + t) % 8, k == 0, k == KD - 1)
                        if t == NT - 1 and k % 2 == 1 and k < KD - 1:
                            ins.then_inc(unit_done, 1)
                    ins.then_inc(w_done, 1)
                    if t == NT - 1:
                        pe.drain().then_inc(unit_done, 1)
                if t > 0:
                    if t == 1:
                        pe.wait_ge(h_up, NT)
                    else:
                        pe.wait_ge(y_done, NT + t - 1)
                    transposes(hxn, 4, t - 1, NT)

            def ffn(u0, f0, steps):
                with pe.Fori(0, steps) as i2:
                    for ff in range(2):
                        n = u0 + 4 * i2 + 2 * ff
                        f = f0 + 2 * i2 + ff
                        pe.wait_ge(u_free, f + 1)
                        for i in range(6):
                            part(n, 2 * ff, 6, i)
                        pe.wait_ge(v_free, f + 1)
                        for i in range(6):
                            part(n + 1, 2 * ff + 1, 0, i)

            def down(u0, u1, tiles, f_done, base, by_token):
                mid = (u0 + u1) // 2
                for half in range(2):
                    for n in range(u0 if half == 0 else mid, mid if half == 0 else u1 - by_token):
                        pe.wait_ge(lo_split, n + 1)
                        first = n in (u0, mid)
                        last = n + 1 in (mid, u1)
                        if first and half == 0:
                            pe.wait_ge(u_free, f_done + 1)
                        if first and half == 1:
                            pe.wait_ge(v_free, f_done + 1)
                        for k2 in range(2):
                            k = 2 * (n - (u0, mid)[half]) + k2
                            if half == 0:
                                pe.wait_ge(g_lo, f_done - tiles + k + 1)
                            for t in range(NT):
                                if first and k2 == 0 and half == 1 and t >= 2:
                                    pe.wait_ge(h_up, base + t - 1)
                                ins = rows(n, k2, g, k, t, (2 + t, t)[half], first and k2 == 0, last and k2 == 1)
                                if last and k2 == 1:
                                    ins.then_inc(dn, 1)
                        pe.drain().then_inc(unit_done, 1)
                for t in range(NT if by_token else 0):
                    for n in range(u1 - by_token, u1):
                        if t == 0:
                            pe.wait_ge(lo_split, n + 1)
                        for k2 in range(2):
                            ins = rows(n, k2, g, 2 * (n - mid) + k2, t, t, False, n == u1 - 1 and k2 == 1)
                    ins.then_inc(dn, 1)

            pe.wait_ge(ylo_done, 2 * NT)
            pe.wait_ge(h_up, 2 * NT)
            ffn(U_FA, 0, FA // 2)
            down(U_DA, U_FB, FA, FA, 2 * NT, 0)
            pe.wait_ge(h_up, 4 * NT)
            ffn(U_FB, FA, (NF - FA) // 2)
            down(U_DB, UNITS, NF - FA, NF, 4 * NT, 4)


def _tables():
    f32 = np.float32
    half = DK_R // 2
    inv = (f32(10000.0) ** (-np.arange(half, dtype=f32) / f32(half))).astype(f32)
    pos = np.concatenate([np.arange(NS), np.arange(NP)]).astype(f32)
    ang = (pos[:, None] * inv[None, :]).astype(f32).astype(np.float64)
    cos, sin = np.cos(ang).T, np.sin(ang).T
    rot = np.empty((P, 2, T), f32)
    for q in range(4):
        rot[32 * q:32 * q + 32, 0] = cos
        rot[32 * q:32 * q + 32, 1] = -sin if q % 2 == 0 else sin
    gamma = 1.0 - 2.0 ** (-5.0 - np.arange(HEADS_R))
    dist = np.abs(np.arange(STRIP)[None, :] - np.arange(P)[:, None] - 3 * P)
    strip = (DK_R ** -0.5 * gamma[:, None, None] ** dist[None]).astype(f32)
    strips = np.ascontiguousarray(strip.reshape(PAIRS, 2, P, STRIP).transpose(0, 2, 1, 3)).reshape(PAIRS, P, 2 * STRIP)
    i = np.arange(P)
    masks = np.stack([((i[:, None] // s) ^ 1) == (i[None, :] // s) for s in LEVELS[:7]], 1).astype(f32)
    sel = np.zeros((P, KD, NH), f32)
    selT = np.zeros((NH, KD, P), f32)
    for tile in range(KD):
        for p in range(P):
            head = 2 * tile + p // DK_R if tile < PAIRS else HEADS_R + tile - PAIRS
            sel[p, tile, head] = 1.0 / (DK_R if tile < PAIRS else P)
            selT[head, tile, p] = 1.0
    return rot, np.ascontiguousarray(masks), strips, sel, selT


def _units(w_in, w_ret_up, w_hg_up, w_out, w_ffn_in, w_ffn_down):
    def cols(w, c0):
        return w[:, c0:c0 + P].reshape(KD, P, P).transpose(1, 0, 2).reshape(P, UNIT)

    def rows(w, k, half):
        return w[2 * k * P:2 * (k + 1) * P, 512 * half:512 * half + 512].reshape(2, P, 512).transpose(1, 0, 2).reshape(P, UNIT)

    rq, rk, rv, rg, hq, ff, fb, hi, hg, ga, gb = 0, 512, 1024, 1536, 2048, 2560, 3072, 3584, 4096, 4608, 5632
    out = []
    for i in range(HEADS_H):
        out += [cols(w_in, c + i * P) for c in (ff, fb, hq, hi, rq, rk, rv, rg)]
    out += [cols(w_in, hg + i * P) for i in range(HEADS_H)]
    up = np.concatenate([w_ret_up, w_hg_up], 0)
    for j in range(KD):
        out += [cols(w_in, ga + j * P), cols(w_in, gb + j * P), cols(up, j * P)]
    out += [rows(w_out, k, half) for half in range(2) for k in range(KD // 2)]
    for f0, f1 in ((0, FA), (FA, NF)):
        for f in range(f0, f1):
            out += [cols(w_ffn_in, f * P), cols(w_ffn_in, FF + f * P)]
        out += [rows(w_ffn_down, k, half) for half in range(2) for k in range(f0 // 2, f1 // 2)]
    assert len(out) == UNITS
    return np.stack(out)


def kernel(**inputs):
    from concourse import bacc
    from concourse.bass_utils import run_bass_kernel_spmd

    a = {k: np.asarray(v) for k, v in inputs.items()}
    rot, masks, strips, sel, selT = _tables()
    tiles = lambda v: v.reshape(-1, P).T
    vec = np.concatenate(
        [tiles(a["norm_mix"][0]), tiles(a["norm_ffn"][0]), tiles(a["w_ret_norm"][0]), tiles(a["w_hg_norm"][0])]
        + [tiles(a["conv_w"][0, i]) for i in range(3)] + [tiles(a["conv_b"][0])]
        + [tiles(a["lower_bounds"][r, d]) for r in range(2) for d in range(2)], 1)
    arrays = {
        "x_s": a["x_sample"][0], "x_p": a["x_prompt"][0],
        "units": _units(a["w_in"][0], a["w_ret_up"][0], a["w_hg_up"][0], a["w_out"][0], a["w_ffn_in"][0], a["w_ffn_down"][0]),
        "vec": vec, "w_final": np.broadcast_to(a["norm_final"][None, :], (P, D)),
        "ident": np.eye(P, dtype=np.float32), "masks": masks, "rot": rot, "strips": strips, "sel": sel, "selT": selT,
    }
    arrays = {f"in_{k}": np.ascontiguousarray(v) for k, v in arrays.items()}
    nc = bacc.Bacc("TRN2", target_bir_lowering=False, num_devices=1, dynamic_dma_scratch_size=1024)
    args = [nc.dram_tensor(k, v.shape, mybir.dt.from_np(v.dtype), kind="ExternalInput").ap() for k, v in arrays.items()]
    outs = [nc.dram_tensor(k, [n, D], F32, kind="ExternalOutput").ap() for k, n in (("y_s", NS), ("y_p", NP))]
    build(nc, *args, *outs)
    r = run_bass_kernel_spmd(nc, [arrays], core_ids=[0]).results[0]
    return r["y_p"].reshape(1, NP, D), r["y_s"].reshape(1, NS, D)
```

```python
from contextlib import ExitStack

import numpy as np

import concourse.bass as bass
from concourse import mybir

ALU = mybir.AluOpType
ACT = mybir.ActivationFunctionType
F32 = mybir.dt.float32
F32R = mybir.dt.float32r
U32 = mybir.dt.uint32

P = 128
D = 1024
KD = D // P
NS, NP = 512, 256
T = NS + NP
NT = T // P
GROUPS = ((0, NS), (NS, NP))
HEADS_R, DK_R = 8, 64
PAIRS = HEADS_R // 2
HEADS_H = 4
FF = 2816
NF = FF // P
EPS = 1e-6
STRIP = NS + 3 * P
FA = 12
UNIT = 1024

U_MIX = 8
U_HG = U_MIX * HEADS_H
U_UP = U_HG + HEADS_H
U_O0 = U_UP + 3 * KD
U_O1 = U_O0 + 4
U_FA = U_O1 + 4
U_DA = U_FA + 2 * FA
U_FB = U_DA + FA
U_DB = U_FB + 2 * (NF - FA)
UNITS = U_DB + NF - FA

V_MIX, V_FFN, V_GATE, V_CONV, V_LB = 0, 8, 16, 24, 24 + 4 * NF
V_N = V_LB + 16

LEVELS = [1 << i for i in range(9)]
JOBS = ["hoT", "roT", "diag", 1, 2, 4, "hgT", 8, 16, 32, 64, 128, 256, "hgPV", "rvT"]
MERGED = ["roT", "diag", 1, 2, 4, 8, 16, 32, 64]
MOVED = ["hoT", "hgT", 128, 256, "hgPV", "rvT"]
GATED = [0, 1, 2, 4, 5, 6, 3, 7]


def strided(ap, offset, dims):
    return bass.AP(tensor=ap.tensor, offset=ap.offset + offset, ap=[list(ap.ap[0])] + dims)


def facing(ap, s, t0, n):
    return strided(ap, t0, [[2 * s, n // (2 * s)], [T + s, 2], [1, s]])


def jobs_done(hd, job):
    return len(JOBS) * hd + JOBS.index(job) - 1


def merged_to(hd, job):
    return len(MERGED) * hd + MERGED.index(job)


def moved_to(hd, job):
    return len(MOVED) * hd + MOVED.index(job)


def after(eng, sem, value):
    if not isinstance(value, int) or value > 0:
        eng.wait_ge(sem, value)


def at(i):
    return bass.ds(i, 1)


def build(nc, x_s, x_p, units, vec, w_final, ident_d, masks_d, rot_d, strips_d, y_s, y_p):
    with ExitStack() as ctx:
        def sem(name):
            return ctx.enter_context(nc.semaphore(name))

        def persistent(name, shape, dtype=F32):
            return ctx.enter_context(nc.sbuf_tensor(name, shape, dtype))

        def region(*tensors):
            with ExitStack() as phase:
                return [phase.enter_context(nc.sbuf_tensor(n, s, d)) for n, s, d in tensors]

        raw = persistent("raw", [P, 2, UNIT])
        split = persistent("split", [P, 4, 2, UNIT], F32R)
        hn = persistent("hn", [P, 2, KD, T], F32R)
        ident = persistent("ident", [P, P])
        vecs = persistent("vecs", [P, V_N])
        lb = persistent("lb", [P, 2, 8])
        lbt = persistent("lbt", [P, 3, 8])
        stat = persistent("stat", [P, 4, NT])
        hstat = persistent("hstat", [P, 3, NT + 2 * NT])

        x_in, xn, y32, junk = region(
            ("x_in", [P, NT, D], F32), ("xn0", [P, 2, D], F32), ("y32_0", [P, 2, D], F32), ("junk0", [P, D], F32))
        (oT, kdup, _, rot, masks, rgate, qsplit, otok, tree_t, tree_q, tree_k, qh, yc, pt, vT, hv, swp,
         sig, qT, klow, rv, strips) = region(
            ("oT", [P, KD, T], F32), ("kdup", [P, 2, T], F32R), ("gap0", [P, 2048 - 2 * T], F32), ("rot", [P, 2, T], F32),
            ("masks", [P, 7, P], F32), ("rgate", [P, T], F32), ("qsplit", [P, 2, T], F32R), ("otok", [P, 2, T], F32),
            ("tree_t", [P, 4 * T], F32), ("tree_q", [P, 2, T], F32), ("tree_k", [P, 2, T], F32),
            ("qh", [P, T], F32), ("yc", [P, T], F32), ("pt", [P, 4 * NS + 2 * NP], F32),
            ("vT", [P, T], F32), ("hv", [P, T], F32), ("swp", [P, T], F32),
            ("sig", [P, 2, T], F32), ("qT", [P, T], F32), ("klow", [P, T], F32R), ("rv", [P, T], F32),
            ("strips", [P, 2, STRIP], F32))
        _, osq, _, kT = region(
            ("d0", [P, KD * T + 2048 + 2 * T + 7 * P + T], F32), ("osq", [P, 2, T], F32),
            ("d1", [P, 18 * T + 4 * NS + 2 * NP], F32), ("kT", [P, T], F32))
        *_, gated, _, _, tg = region(
            ("a0", [P, KD, T], F32), ("a1", [P, 2048], F32), ("a2", [P, 2, T], F32), ("a3", [P, 7, P], F32),
            ("a4", [P, T], F32), ("a5", [P, 2, T], F32), ("a6", [P, 2, T], F32),
            ("gated", [P, 2, KD, T], F32R), ("a7", [P, 256], F32), ("a8", [P, 2, T], F32), ("tg", [P, 2, T], F32))
        (merged,) = region(("merged", [P, 2, KD, T], F32R))
        _, h, hxn, hy32, hjunk, wfin = region(
            ("b0", [P, 2 * FA * T], F32), ("h", [P, NT, D], F32), ("hxn", [P, 2, D], F32),
            ("hy32", [P, 2, D], F32), ("hjunk", [P, D], F32), ("wfin", [P, D], F32))
        g, _, cb, gl, g32 = region(
            ("g", [P, 2, FA, T], F32R), ("c0", [P, NT * D], F32), ("cb", [P, T], F32),
            ("gl", [P, T], F32), ("g32", [P, T], F32))

        ps = ctx.enter_context(nc.psum_tensor("ps", [P, 8, 512], F32))
        psf = ps[:].rearrange("p b n -> p (b n)")

        x_ld = [sem(f"x_loaded{t}") for t in range(NT)]
        raw_ld = [sem("raw0_loaded"), sem("raw1_loaded")]
        vec_ld, mix_ld, strip_ld, fin_ld, out_st = sem("vec_loaded"), sem("mix_loaded"), sem("strip_loaded"), sem("fin_loaded"), sem("out_stored")
        h_ld = sem("h_loaded")
        hi_split, lo_split, unit_done = sem("hi_split"), sem("lo_split"), sem("unit_done")
        dfree = [sem("dense0_free"), sem("dense1_free")]
        sq_done, var_done, sd_done, xn_done, tr_done, y_done, yhi_done, ylo_done = (
            sem(n) for n in ("sq_done", "var_done", "sd_done", "xn_done", "tr_done", "y_done", "yhi_done", "ylo_done"))
        seeded = sem("root_seeded")
        lb_max, lb_exp = sem("lb_max"), sem("lb_exp")
        sg, sc = sem("sigmoid_done"), sem("sigmoid_used")
        vt_done, swap_done, rot_done = sem("vT_done"), sem("swap_done"), sem("rotary_done")
        kq_hi, kq_lo = sem("ret_hi"), sem("ret_lo")
        rs, rp, rpv, ro = sem("ret_scores"), sem("ret_decayed"), sem("ret_pv"), sem("ret_out")
        qk_done, q_up, k_up, yc_done = sem("qk_done"), sem("q_updated"), sem("k_updated"), sem("yc_done")
        mj, mg, mv = sem("mixer_job"), sem("mixer_merged"), sem("mixer_moved")
        sqh, veps, sdh, normed, ghi, glo = (
            sem(n) for n in ("head_sq", "head_var", "head_sd", "head_normed", "gated_hi", "gated_lo"))
        upf, m32, mhi, mlo = sem("up_free"), sem("merged32"), sem("merged_hi"), sem("merged_lo")
        w_done, h_up = sem("wout_done"), sem("h_updated")
        u_free, v_free, c_done, conv_done, gelu_done, g32_done, g_hi, g_lo = (
            sem(n) for n in ("u_free", "v_free", "centre_done", "conv_done", "gelu_done", "g32_done", "g_hi", "g_lo"))
        dn, out_rdy = sem("down_done"), sem("out_ready")

        blk = ctx.enter_context(nc.Block())

        @blk.sync
        def _(sp):
            def load(n, parity):
                after(sp, lo_split, n - 1)
                src = units[n] if isinstance(n, int) else units[at(n), :, :].rearrange("a p n -> (a p) n")
                sp.dma_start(raw[:, parity, :], src).then_inc(raw_ld[parity], 16)

            xs = x_s.rearrange("(t p) d -> t p d", p=P)
            xp = x_p.rearrange("(t p) d -> t p d", p=P)
            for t in range(NT):
                sp.dma_start(x_in[:, t, :], xs[t] if t < 4 else xp[t - 4]).then_inc(x_ld[t], 16)

            def mixer_loads(hd):
                for u in range(U_MIX):
                    load(hd * U_MIX + u, u % 2)
                    if u == 5:
                        after(sp, rp, 12 * hd)
                        src = strips_d[hd] if isinstance(hd, int) else strips_d[at(hd), :, :].rearrange("a p n -> (a p) n")
                        sp.dma_start(strips[:].rearrange("p a n -> p (a n)"), src).then_inc(strip_ld, 16)

            mixer_loads(0)
            with sp.Fori(1, HEADS_H) as hd:
                mixer_loads(hd)
            with sp.Fori(U_HG // 2, (U_O0 + 4) // 2) as i:
                load(2 * i, 0)
                load(2 * i + 1, 1)
            sp.wait_ge(unit_done, U_O0)
            sp.dma_start(h[:, 0:4, :], x_s.rearrange("(t p) d -> p t d", p=P)).then_inc(h_ld, 16)
            sp.dma_start(h[:, 4:6, :], x_p.rearrange("(t p) d -> p t d", p=P)).then_inc(h_ld, 16)
            sp.wait_ge(mlo, KD)
            sp.dma_start(wfin[:], w_final).then_inc(fin_ld, 16)
            with sp.Fori((U_O0 + 4) // 2, UNITS // 2) as i:
                load(2 * i, 0)
                load(2 * i + 1, 1)
            ys = y_s.rearrange("(t p) d -> t p d", p=P)
            yp = y_p.rearrange("(t p) d -> t p d", p=P)
            for t in range(NT):
                sp.wait_ge(out_rdy, t + 1)
                sp.dma_start(ys[t] if t < 4 else yp[t - 4], h[:, t, :]).then_inc(out_st, 16)
            sp.wait_ge(out_st, 16 * NT)

        @blk.scalar
        def _(act):
            act.dma_start(vecs[:], vec).then_inc(vec_ld, 16)
            act.dma_start(ident[:], ident_d).then_inc(vec_ld, 16)

            def split_hi(n, slot):
                after(act, raw_ld[slot % 2], 8 * (n - slot % 2) + 16)
                after(act, unit_done, n - 3)
                act.activation(split[:, slot, 0, :], raw[:, slot % 2, :], ACT.Copy).then_inc(hi_split, 1)

            def square(src, t, base, out):
                act.drain()
                act.activation(out, src, ACT.Square, accum_out=stat[:, 0, t:t + 1]).then_inc(sq_done, 1)

            def sqrt(t, base):
                act.wait_ge(var_done, base + t + 1)
                act.activation(stat[:, 2, t:t + 1], stat[:, 1, t:t + 1], ACT.Sqrt).then_inc(sd_done, 1)

            def norm_hi(t, base, y):
                act.wait_ge(y_done, base + t + 1)
                act.activation(hn[:, 0, :, t * P:(t + 1) * P], y[:, t % 2, :].rearrange("p (k n) -> p k n", k=KD),
                               ACT.Copy).then_inc(yhi_done, 1)

            act.wait_ge(seeded, 1)
            act.activation(hstat[:, 1, 0:1], hstat[:, 0, 0:1], ACT.Sqrt)
            for t in range(-3, NT):
                if t + 3 < NT:
                    act.wait_ge(x_ld[t + 3], 16)
                    square(x_in[:, t + 3, :], t + 3, 0, junk[:])
                if 0 <= t + 2 < NT:
                    sqrt(t + 2, 0)
                if t >= 0:
                    norm_hi(t, 0, y32)
                if t in (0, 1):
                    split_hi(t, t)
            act.wait_ge(yhi_done, NT)
            act.wait_ge(ylo_done, NT)
            act.dma_start(rot[:], rot_d).then_inc(mix_ld, 16)
            act.dma_start(masks[:], masks_d).then_inc(mix_ld, 16)
            act.wait_ge(lb_max, 1)
            act.activation(lbt[:, 0:2, :], lb[:], ACT.Exp).then_inc(lb_exp, 1)

            def dense(u):
                return ps[:, 2 * (u % 2):2 * (u % 2) + 2, :].rearrange("p b n -> p (b n)")[:, 0:T]

            def pair(j):
                return ps[:, 4 + 2 * (j % 2):6 + 2 * (j % 2), :].rearrange("p b n -> p (b n)")

            def sigmoid(n, i, u):
                act.wait_ge(unit_done, n + 1)
                after(act, sc, i - 2)
                ins = act.activation(sig[:, u % 2, :], dense(u), ACT.Sigmoid)
                ins.then_inc(sg, 1)
                return ins

            def free_dense(u):
                act.drain().then_inc(dfree[u % 2], 1)

            def copy_y(hd, level):
                i = level.bit_length() - 1
                act.wait_ge(k_up, 9 * hd + 1 + i)
                act.wait_ge(mj, jobs_done(hd, "diag" if i == 0 else LEVELS[i - 1]))
                act.activation(strided(yc[:], 0, [[2 * level, T // (2 * level)], [level, 2], [1, level]]),
                               facing(tree_k[:], level, 0, T), ACT.Copy).then_inc(yc_done, 1)

            def swap(hd, u, i):
                act.wait_ge(unit_done, U_MIX * hd + u + 1)
                after(act, rot_done, 2 * hd + i)
                for q in range(4):
                    to = (q ^ 1) * 32
                    ins = act.activation(swp[to:to + 32, :], dense(u)[q * 32:q * 32 + 32, :], ACT.Copy)
                ins.then_inc(swap_done, 1)

            def turn_v(hd, u, job_before):
                act.wait_ge(unit_done, U_MIX * hd + u + 1)
                after(act, mj, job_before)
                act.activation(vT[:], dense(u), ACT.Copy).then_inc(vt_done, 1)
                free_dense(u)

            def move(hd, job):
                act.wait_ge(mj, jobs_done(hd, job))
                src = pair(JOBS.index(job))
                if job == "hgT":
                    act.activation(hv[:], src[:, 0:T], ACT.Copy).then_inc(mv, 1)
                elif job == "rvT":
                    act.activation(rv[:], src[:, 0:T], ACT.Copy).then_inc(mv, 1)
                elif job == "hgPV":
                    act.activation(otok[:, 0, :], src[:, 0:T], ACT.Copy).then_inc(mv, 1)
                elif job == "hoT":
                    tile = hd + HEADS_H - 1
                    dst, src, w = (oT[:, tile, :], src[:, 0:T], vecs[:, V_GATE + tile:V_GATE + tile + 1]) if isinstance(hd, int) else (
                        oT[:, at(tile), :], src[:, None, 0:T], vecs[:, bass.ds(V_GATE + tile, 1)])
                    act.activation(dst, src, ACT.Copy, scale=w).then_inc(mv, 1)
                elif job == 128:
                    for off, m in ((P, 0), (NS, 1)):
                        act.activation(strided(pt[:], off, [[2 * NS + 2 * P, 2], [1, P]]),
                                       strided(src, m * P, [[2 * P, 2], [1, P]]), ACT.Copy)
                    act.activation(pt[:, 4 * NS + P:4 * NS + 3 * P], src[:, NS:NS + 2 * P], ACT.Copy).then_inc(mv, 1)
                else:
                    act.activation(strided(pt[:], 2 * P, [[NS, 2], [1, 2 * P]]),
                                   strided(src, 0, [[2 * P, 2], [1, 2 * P]]), ACT.Copy)
                    act.activation(strided(pt[:], 2 * NS, [[NS, 2], [1, 2 * P]]),
                                   strided(src, 4 * P, [[2 * P, 2], [1, 2 * P]]), ACT.Copy).then_inc(mv, 1)

            def ret_hi(hd):
                act.wait_ge(rot_done, 2 * hd + 2)
                after(act, rpv, 12 * hd)
                for a in range(2):
                    own = slice(64 * a, 64 * a + 64)
                    for to in (0, 64):
                        act.activation(kdup[to:to + 64, a, :], kT[own, :], ACT.Copy)
                    ins = act.activation(qsplit[own, a, :], qT[own, :], ACT.Copy)
                ins.then_inc(kq_hi, 1)

            def ret_out(pr):
                act.wait_ge(rpv, 12 * pr + 12)
                act.activation(otok[:, 1, :], pair(1)[:, 0:T], ACT.Copy).then_inc(ro, 1)
                act.drain()
                act.activation(osq[:], otok[:], ACT.Square).then_inc(sqh, 1)

            def head_sqrt(pr):
                act.wait_ge(veps, pr + 1)
                act.activation(hstat[:, 1, :], hstat[:, 0, :], ACT.Sqrt).then_inc(sdh, 1)

            def mixer(hd, first):
                n = U_MIX * hd
                if not first:
                    sigmoid(n - 1, 4 * hd, 7)
                split_hi(n + 2, 2)
                sigmoid(n, 4 * hd + 1, 0)
                free_dense(0)
                split_hi(n + 3, 3)
                sigmoid(n + 1, 4 * hd + 2, 1)
                free_dense(1)
                split_hi(n + 4, 0)
                if not first:
                    ret_out(hd - 1)
                    head_sqrt(hd - 1)
                sigmoid(n + 2, 4 * hd + 3, 2)
                split_hi(n + 5, 1)
                if not first:
                    move(hd, "hoT")
                copy_y(hd, 1)
                turn_v(hd, 3, 0 if first else jobs_done(hd - 1, "rvT"))
                copy_y(hd, 2)
                split_hi(n + 6, 2)
                copy_y(hd, 4)
                swap(hd, 4, 0)
                copy_y(hd, 8)
                move(hd, "hgT")
                split_hi(n + 7, 3)
                copy_y(hd, 16)
                copy_y(hd, 32)
                swap(hd, 5, 1)
                copy_y(hd, 64)
                split_hi(n + 8, 0)
                ret_hi(hd)
                turn_v(hd, 6, jobs_done(hd, "hgT"))
                after(act, rpv, 12 * hd)
                move(hd, 128)
                split_hi(n + 9, 1)
                for job in (256, "hgPV", "rvT"):
                    move(hd, job)

            mixer(0, True)
            with act.Fori(1, HEADS_H) as hd:
                mixer(hd, False)

            sigmoid(U_HG - 1, 16, 7)
            split_hi(U_HG + 2, 2)
            sigmoid(U_HG, 17, 0)
            split_hi(U_HG + 3, 3)
            sigmoid(U_HG + 1, 18, 1)
            split_hi(U_HG + 4, 0)
            ret_out(PAIRS - 1)
            head_sqrt(PAIRS - 1)
            sigmoid(U_HG + 2, 19, 0)
            split_hi(U_HG + 5, 1)
            move(HEADS_H, "hoT")
            for i, tile in enumerate(GATED):
                if i == 6:
                    sigmoid(U_HG + 3, 20, 1)
                if tile < PAIRS:
                    act.wait_ge(mg, merged_to(tile + 1, "roT"))
                else:
                    act.wait_ge(sc, 17 + tile - PAIRS)
                act.activation(gated[:, 0, tile, :], oT[:, tile, :], ACT.Copy).then_inc(ghi, 1)

            with act.Fori(0, 2) as i2:
                for jj in range(4):
                    n = U_UP + 12 * i2 + 3 * jj
                    j = 4 * i2 + jj
                    split_hi(n + 2, (3 * jj + 2) % 4)
                    sigmoid(n, 20 + 2 * j + 1, 0)
                    free_dense(0)
                    split_hi(n + 3, (3 * jj + 3) % 4)
                    sigmoid(n + 1, 20 + 2 * j + 2, 1)
                    free_dense(1)
                    split_hi(n + 4, (3 * jj + 4) % 4)
                    act.wait_ge(m32, j + 1)
                    act.activation(merged[:, 0, at(j), :], tg[:, None, 0, :], ACT.Copy).then_inc(mhi, 1)

            for n in range(U_O0, U_O1):
                split_hi(n + 2, (n + 2) % 4)
            split_hi(U_O1 + 2, 2)
            split_hi(U_O1 + 3, 3)
            for t in range(NT + 1):
                if t < NT:
                    act.wait_ge(h_up, NT + t + 1)
                    square(h[:, t, :], t, NT, hjunk[:])
                    sqrt(t, NT)
                if t > 0:
                    norm_hi(t - 1, NT, hy32)
                if t == NT - 2:
                    split_hi(U_FA, 0)
                    split_hi(U_FA + 1, 1)

            def ffn(u0, f0, steps):
                with act.Fori(0, steps) as i:
                    for ff in range(2):
                        n = u0 + 4 * i + 2 * ff
                        f = f0 + 2 * i + ff
                        split_hi(n + 2, (2 * ff + 2) % 4)
                        act.wait_ge(unit_done, n + 1)
                        act.activation(cb[:], psf[:, 6 * 512:6 * 512 + T], ACT.Identity,
                                       bias=vecs[:, bass.ds(V_CONV + 3 * NF + f, 1)],
                                       scale=vecs[:, bass.ds(V_CONV + NF + f, 1)]).then_inc(c_done, 1)
                        split_hi(n + 3, (2 * ff + 3) % 4)
                        act.wait_ge(conv_done, f + 1)
                        act.activation(gl[:], cb[:], ACT.Gelu_apprx_tanh).then_inc(gelu_done, 1)
                        act.wait_ge(g32_done, f + 1)
                        act.activation(g[:, 0, at(2 * i + ff), :], g32[:, None, :], ACT.Copy).then_inc(g_hi, 1)

            ffn(U_FA, 0, FA // 2)
            for n in range(U_DA, U_FB):
                split_hi(n + 2, (n + 2) % 4)
            act.wait_ge(unit_done, U_FB)
            ffn(U_FB, FA, (NF - FA) // 2)
            for n in range(U_DB, UNITS - 2):
                split_hi(n + 2, (n + 2) % 4)
            for t in range(NT):
                act.wait_ge(h_up, 5 * NT + t + 1)
                square(h[:, t, :], t, 2 * NT, hjunk[:])
                sqrt(t, 2 * NT)

        @blk.vector
        def _(dve):
            def split_lo(n, slot):
                after(dve, hi_split, n + 1)
                dve.tensor_tensor(split[:, slot, 1, :], raw[:, slot % 2, :], split[:, slot, 0, :].bitcast(F32),
                                  ALU.subtract).then_inc(lo_split, 1)

            def variance(t, base):
                dve.wait_ge(sq_done, base + t + 1)
                dve.tensor_scalar(stat[:, 1, t:t + 1], stat[:, 0, t:t + 1], 1.0 / D, EPS, ALU.mult,
                                  ALU.add).then_inc(var_done, 1)

            def scale(src, t, base, out):
                dve.wait_ge(sd_done, base + t + 1)
                dve.reciprocal(stat[:, 3, t:t + 1], stat[:, 2, t:t + 1])
                dve.drain()
                if t >= 2:
                    dve.wait_ge(tr_done, base + t - 1)
                dve.tensor_scalar(out[:, t % 2, :], src, stat[:, 3, t:t + 1], None, ALU.mult).then_inc(xn_done, 1)

            def weigh(t, base, col, bank, y):
                dve.wait_ge(tr_done, base + t + 1)
                y = y[:, t % 2, :].rearrange("p (k n) -> p k n", k=KD)
                dve.tensor_tensor(y,
                                  ps[:, bank:bank + 2, :].rearrange("p b (k n) -> p (b k) n", n=P),
                                  vecs[:, col:col + KD, None].broadcast_to([P, KD, P]), ALU.mult).then_inc(y_done, 1)

            def norm_low(t, base, y):
                dve.wait_ge(yhi_done, base + t + 1)
                y = y[:, t % 2, :].rearrange("p (k n) -> p k n", k=KD)
                dve.tensor_tensor(hn[:, 1, :, t * P:(t + 1) * P], y,
                                  hn[:, 0, :, t * P:(t + 1) * P].bitcast(F32), ALU.subtract).then_inc(ylo_done, 1)
                dve.drain()

            dve.memset(hstat[:, 0, 0:1], 1.0).then_inc(seeded, 1)
            dve.wait_ge(vec_ld, 32)
            for t in range(-2, NT + 1):
                if t + 2 < NT:
                    variance(t + 2, 0)
                if 0 <= t + 1 < NT:
                    scale(x_in[:, t + 1, :], t + 1, 0, xn)
                if 0 <= t < NT:
                    weigh(t, 0, V_MIX, 4 + 2 * (t % 2), y32)
                if t > 0:
                    norm_low(t - 1, 0, y32)
                if t in (1, 2):
                    split_lo(t - 1, t - 1)
            lrow = vecs[:, V_LB:V_LB + 16].rearrange("p (r c) -> p r c", r=2)
            dve.tensor_tensor(lbt[:, 2, :], lrow[:, 0, :], lrow[:, 1, :], ALU.max)
            dve.drain()
            dve.tensor_tensor(lb[:], lrow, lbt[:, 2:3, :].broadcast_to([P, 2, 8]), ALU.subtract).then_inc(lb_max, 1)
            dve.wait_ge(lb_exp, 1)
            dve.tensor_tensor(lbt[:, 2, :], lbt[:, 0, :], lbt[:, 1, :], ALU.add)
            dve.drain()
            dve.reciprocal(lbt[:, 1, :], lbt[:, 2, :])
            dve.drain()
            dve.tensor_tensor(lb[:, 0, :], lbt[:, 0, :], lbt[:, 1, :], ALU.mult)
            dve.drain()
            dve.tensor_scalar(lb[:, 1, :], lb[:, 0, :], -1.0, 1.0, ALU.mult, ALU.add)
            dve.drain()

            def dense(u):
                return ps[:, 2 * (u % 2):2 * (u % 2) + 2, :].rearrange("p b n -> p (b n)")[:, 0:T]

            def pair(j):
                return ps[:, 4 + 2 * (j % 2):6 + 2 * (j % 2), :].rearrange("p b n -> p (b n)")

            def decay(pr, i):
                a, m = divmod(i, 6)
                dve.wait_ge(rs, 12 * pr + i + 1)
                if i >= 4:
                    dve.wait_ge(rpv, 12 * pr + i - 3)
                width = NS if m < 4 else NP
                c0 = STRIP - NS - P * (m % 4)
                dve.tensor_tensor(pt[:, (i % 4) * NS:(i % 4) * NS + width], ps[:, 4 + i % 2, 0:width],
                                  strips[:, a, c0:c0 + width], ALU.mult).then_inc(rp, 1)

            def ret_gate(i, u):
                dve.wait_ge(sg, i)
                dve.tensor_tensor(rgate[:], dense(u), sig[:, u % 2, :], ALU.mult).then_inc(sc, 1)
                dve.drain().then_inc(dfree[u % 2], 1)

            def hg_gate(hd, u):
                dve.wait_ge(sg, 17 + hd)
                dve.tensor_tensor(sig[:, u % 2, :], dense(u), sig[:, u % 2, :], ALU.mult)
                dve.drain().then_inc(dfree[u % 2], 1)
                dve.wait_ge(mv, moved_to(hd + 1, "hoT"))
                dve.tensor_tensor(oT[:, HEADS_H + hd, :], oT[:, HEADS_H + hd, :], sig[:, u % 2, :], ALU.mult).then_inc(sc, 1)

            groups = ((otok[:, 0, :].rearrange("p (c e) -> p c e", e=P), osq[:, 0, :].rearrange("p (c e) -> p c e", e=P), 0, NT, P),
                      (otok[:, 1, :].rearrange("p (c e) -> p c e", e=DK_R), osq[:, 1, :].rearrange("p (c e) -> p c e", e=DK_R), NT, 3 * NT, DK_R))

            def head_squares(pr):
                dve.wait_ge(sqh, pr + 1)
                for _, square, c0, c1, _ in groups:
                    dve.tensor_reduce(hstat[:, 2, c0:c1], square, mybir.AxisListType.X, ALU.add)
                dve.drain()
                for _, _, c0, c1, width in groups:
                    ins = dve.tensor_scalar(hstat[:, 0, c0:c1], hstat[:, 2, c0:c1], 1.0 / width, EPS, ALU.mult, ALU.add)
                ins.then_inc(veps, 1)

            def head_norm(pr):
                dve.wait_ge(sdh, pr + 1)
                dve.reciprocal(hstat[:, 2, :], hstat[:, 1, :])
                dve.drain()
                for out, _, c0, c1, width in groups:
                    dve.tensor_tensor(out, out, hstat[:, 2, c0:c1, None].broadcast_to([P, c1 - c0, width]),
                                      ALU.mult).then_inc(normed, 1)

            def ret_finish(hd):
                dve.wait_ge(mj, jobs_done(hd, "roT"))
                pr = hd - 1
                if isinstance(hd, int):
                    dve.scalar_tensor_tensor(out=oT[:, pr, :], in0=pair(1)[:, 0:T], scalar=vecs[:, V_GATE + pr:V_GATE + hd],
                                             in1=rgate[:], op0=ALU.mult, op1=ALU.mult).then_inc(mg, 1)
                else:
                    dve.scalar_tensor_tensor(out=oT[:, at(pr), :], in0=pair(1)[:, None, 0:T],
                                             scalar=vecs[:, bass.ds(V_GATE + pr, 1)], in1=rgate[:, None, :],
                                             op0=ALU.mult, op1=ALU.mult).then_inc(mg, 1)
                dve.drain()

            def forget(hd, d):
                c = 4 * d + hd
                cols = (lb[:, 1, c:c + 1], lb[:, 0, c:c + 1]) if isinstance(c, int) else (lb[:, 1, at(c)], lb[:, 0, at(c)])
                dve.wait_ge(sg, 4 * hd + 1 + d)
                f = tree_t[:, (1 - d) * T:(2 - d) * T]
                dve.tensor_scalar(f, sig[:, d, :], cols[0], cols[1], ALU.mult, ALU.add).then_inc(sc, 1)
                dve.drain()
                ins = dve.tensor_scalar(tree_k[:, d, :], f, -1.0, 1.0, ALU.mult, ALU.add)
                if d == 1:
                    ins.then_inc(k_up, 1)

            def queries(hd):
                dve.wait_ge(sg, 4 * hd + 3)
                dve.tensor_tensor(qh[:], dense(2), sig[:, 0, :], ALU.mult).then_inc(sc, 1)
                dve.drain().then_inc(dfree[0], 1)
                dve.tensor_tensor(tree_q[:], qh[:, None, :].broadcast_to([P, 2, T]),
                                  tree_t[:, 0:2 * T].rearrange("p (a n) -> p a n", a=2), ALU.mult).then_inc(q_up, 1)
                dve.tensor_tensor(yc[:], tree_k[:, 0, :], tree_k[:, 1, :], ALU.add).then_inc(qk_done, 1)

            def totals(s):
                return 0 if s == 1 else 4 * T - 4 * T // s

            def update(hd, s):
                i = s.bit_length() - 1
                n = T if s < 128 else NS
                c, nb = totals(s), T // s
                if s < 128:
                    dve.wait_ge(yc_done, 7 * hd + i + 1)
                else:
                    dve.wait_ge(mj, jobs_done(hd, s))
                keys = facing(tree_k[:], s, 0, n)
                dve.tensor_tensor(keys, keys, strided(tree_t[:], c + nb + 1, [[2, n // (2 * s)], [-(nb + 1), 2], [0, s]]),
                                  ALU.mult).then_inc(k_up, 1)
                if s < 128:
                    dve.wait_ge(mj, jobs_done(hd, s))
                qs = facing(tree_q[:], s, 0, n)
                dve.tensor_tensor(qs, qs, strided(tree_t[:], c + 1, [[2, n // (2 * s)], [nb - 1, 2], [0, s]]),
                                  ALU.mult).then_inc(q_up, 1)
                if s < 128:
                    two = strided(tree_t[:], c, [[nb, 2], [2, nb // 2], [1, 2]])
                    dve.tensor_tensor(strided(tree_t[:], totals(2 * s), [[nb // 2, 2], [1, nb // 2]]),
                                      two[:, :, :, 0], two[:, :, :, 1], ALU.mult)
                    dve.drain()

            def merge(hd, job):
                j = JOBS.index(job)
                if job == "diag":
                    dve.wait_ge(mj, jobs_done(hd, job))
                for off, step, c0, nc_ in ((0, NS + P, 0, 4), (4 * NS, NP + P, 4, 2)):
                    dst = strided(pt[:], off, [[step, nc_], [1, P]])
                    src = strided(pair(j), c0 * P, [[P, nc_], [1, P]])
                    if job == "diag":
                        ins = dve.tensor_tensor(dst, src, ident[:, None, :].broadcast_to([P, nc_, P]), ALU.mult)
                    else:
                        ins = dve.copy_predicated(dst, masks[:, LEVELS.index(job):LEVELS.index(job) + 1, :].bitcast(U32).broadcast_to([P, nc_, P]), src)
                ins.then_inc(mg, 1)
                dve.drain()

            def ret_lo(hd):
                dve.wait_ge(kq_hi, hd + 1)
                for a in range(2):
                    own, other = slice(64 * a, 64 * a + 64), slice(64 - 64 * a, 128 - 64 * a)
                    dve.tensor_tensor(qsplit[other, a, :], qT[own, :], qsplit[own, a, :].bitcast(F32), ALU.subtract)
                    ins = dve.tensor_tensor(klow[own, :], kT[own, :], kdup[own, a, :].bitcast(F32), ALU.subtract)
                ins.then_inc(kq_lo, 1)

            def rotary(hd, u, i, dst):
                dve.wait_ge(swap_done, 2 * hd + i + 1)
                dve.tensor_tensor(dst, dense(u), rot[:, 0, :], ALU.mult)
                dve.tensor_tensor(swp[:], swp[:], rot[:, 1, :], ALU.mult)
                dve.drain().then_inc(dfree[u % 2], 1)
                dve.tensor_tensor(dst, dst, swp[:], ALU.add).then_inc(rot_done, 1)

            def mixer(hd, first):
                n = U_MIX * hd
                if not first:
                    ret_gate(4 * hd, 7)
                split_lo(n + 2, 2)
                if not first:
                    dve.wait_ge(strip_ld, 16 * hd)
                    dve.wait_ge(mj, jobs_done(hd - 1, "rvT"))
                    for i in range(6):
                        decay(hd - 1, i)
                forget(hd, 0)
                if not first:
                    for i in range(6, 8):
                        decay(hd - 1, i)
                split_lo(n + 3, 3)
                if not first:
                    for i in range(8, 12):
                        decay(hd - 1, i)
                forget(hd, 1)
                split_lo(n + 4, 0)
                if not first:
                    head_squares(hd - 1)
                    head_norm(hd - 1)
                queries(hd)
                if not first:
                    ret_finish(hd)
                split_lo(n + 5, 1)
                if first:
                    dve.wait_ge(mix_ld, 32)
                after(dve, rpv, 12 * hd)
                merge(hd, "diag")
                update(hd, 1)
                merge(hd, 1)
                split_lo(n + 6, 2)
                update(hd, 2)
                merge(hd, 2)
                update(hd, 4)
                merge(hd, 4)
                after(dve, rs, 12 * hd)
                rotary(hd, 4, 0, qT[:])
                update(hd, 8)
                merge(hd, 8)
                split_lo(n + 7, 3)
                update(hd, 16)
                merge(hd, 16)
                update(hd, 32)
                merge(hd, 32)
                rotary(hd, 5, 1, kT[:])
                update(hd, 64)
                split_lo(n + 8, 0)
                merge(hd, 64)
                update(hd, 128)
                split_lo(n + 9, 1)
                ret_lo(hd)

            mixer(0, True)
            with dve.Fori(1, HEADS_H) as hd:
                mixer(hd, False)

            ret_gate(16, 7)
            split_lo(U_HG + 2, 2)
            dve.wait_ge(strip_ld, 16 * PAIRS)
            dve.wait_ge(mj, jobs_done(HEADS_H - 1, "rvT"))
            for i in range(6):
                decay(PAIRS - 1, i)
            hg_gate(0, 0)
            for i in range(6, 8):
                decay(PAIRS - 1, i)
            split_lo(U_HG + 3, 3)
            for i in range(8, 12):
                decay(PAIRS - 1, i)
            hg_gate(1, 1)
            split_lo(U_HG + 4, 0)
            head_squares(PAIRS - 1)
            head_norm(PAIRS - 1)
            hg_gate(2, 2)
            split_lo(U_HG + 5, 1)
            ret_finish(HEADS_H)
            for i, tile in enumerate(GATED):
                if i == 6:
                    hg_gate(3, 3)
                dve.wait_ge(ghi, i + 1)
                dve.tensor_tensor(gated[:, 1, tile, :], oT[:, tile, :], gated[:, 0, tile, :].bitcast(F32),
                                  ALU.subtract).then_inc(glo, 1)
            dve.drain().then_inc(upf, 1)

            with dve.Fori(0, 2) as i2:
                for jj in range(4):
                    n = U_UP + 12 * i2 + 3 * jj
                    j = 4 * i2 + jj
                    split_lo(n + 2, (3 * jj + 2) % 4)
                    split_lo(n + 3, (3 * jj + 3) % 4)
                    split_lo(n + 4, (3 * jj + 4) % 4)
                    dve.wait_ge(sg, 20 + 2 * j + 2)
                    dve.wait_ge(unit_done, n + 3)
                    dve.tensor_tensor(tg[:, 0, :], psf[:, 4 * 512:4 * 512 + T], sig[:, 0, :], ALU.mult).then_inc(sc, 1)
                    dve.tensor_tensor(tg[:, 1, :], psf[:, 6 * 512:6 * 512 + T], sig[:, 1, :], ALU.mult).then_inc(sc, 1)
                    dve.drain().then_inc(upf, 1)
                    dve.tensor_tensor(tg[:, 0, :], tg[:, 0, :], tg[:, 1, :], ALU.add).then_inc(m32, 1)
                    dve.wait_ge(mhi, j + 1)
                    dve.tensor_tensor(merged[:, 1, at(j), :], tg[:, None, 0, :], merged[:, 0, at(j), :].bitcast(F32),
                                      ALU.subtract).then_inc(mlo, 1)
                    dve.drain()

            def residual(t, half, bank):
                hs = h[:, t, 512 * half:512 * half + 512]
                return dve.tensor_tensor(hs, ps[:, bank, :], hs, ALU.add).then_inc(h_up, 1)

            for n in range(U_O0, U_O1):
                split_lo(n + 2, (n + 2) % 4)
            split_lo(U_O1 + 2, 2)
            dve.wait_ge(h_ld, 32)
            for t in range(NT):
                dve.wait_ge(w_done, t + 1)
                residual(t, 0, t)
            split_lo(U_O1 + 3, 3)
            for t in range(NT + 1):
                if t < NT:
                    dve.wait_ge(w_done, NT + t + 1)
                    residual(t, 1, (6 + t) % 8)
                    if t == 1:
                        dve.drain().then_inc(u_free, 1)
                    if t == 3:
                        dve.drain().then_inc(v_free, 1)
                if t > 0:
                    weigh(t - 1, NT, V_FFN, 4, hy32)
                if t < NT:
                    variance(t, NT)
                    scale(h[:, t, :], t, NT, hxn)
                if t > 0:
                    norm_low(t - 1, NT, hy32)
                if t == NT - 2:
                    split_lo(U_FA, 0)
                    split_lo(U_FA + 1, 1)

            def ffn(u0, f0, steps):
                with dve.Fori(0, steps) as i:
                    for ff in range(2):
                        n = u0 + 4 * i + 2 * ff
                        f = f0 + 2 * i + ff
                        split_lo(n + 2, (2 * ff + 2) % 4)
                        dve.wait_ge(c_done, f + 1)
                        for tap, to, frm in ((0, 1, 0), (2, 0, 1)):
                            for c0, w in GROUPS:
                                cs = cb[:, c0 + to:c0 + to + w - 1]
                                dve.scalar_tensor_tensor(
                                    out=cs, in0=psf[:, 6 * 512 + c0 + frm:6 * 512 + c0 + frm + w - 1],
                                    scalar=vecs[:, bass.ds(V_CONV + tap * NF + f, 1)], in1=cs,
                                    op0=ALU.mult, op1=ALU.add)
                            if tap == 0:
                                dve.drain()
                        dve.drain().then_inc(u_free, 1)
                        dve.drain().then_inc(conv_done, 1)
                        split_lo(n + 3, (2 * ff + 3) % 4)
                        dve.wait_ge(gelu_done, f + 1)
                        dve.wait_ge(unit_done, n + 2)
                        dve.tensor_tensor(g32[:], psf[:, 0:T], gl[:], ALU.mult).then_inc(g32_done, 1)
                        dve.drain().then_inc(v_free, 1)
                        dve.wait_ge(g_hi, f + 1)
                        dve.tensor_tensor(g[:, 1, at(2 * i + ff), :], g32[:, None, :],
                                          g[:, 0, at(2 * i + ff), :].bitcast(F32), ALU.subtract).then_inc(g_lo, 1)

            def down(u0, u1, base):
                mid = (u0 + u1) // 2
                for n in range(u0, u1):
                    if n == mid + 1:
                        for t in range(NT):
                            dve.wait_ge(dn, base + t + 1)
                            residual(t, 0, 2 + t)
                    if n + 2 < UNITS:
                        split_lo(n + 2, (n + 2) % 4)

            ffn(U_FA, 0, FA // 2)
            down(U_DA, U_FB, 0)
            for t in range(NT):
                dve.wait_ge(dn, NT + t + 1)
                residual(t, 1, t)
            ffn(U_FB, FA, (NF - FA) // 2)
            down(U_DB, UNITS, 2 * NT)
            dve.wait_ge(fin_ld, 16)
            for t in range(NT):
                dve.wait_ge(dn, 3 * NT + t + 1)
                residual(t, 1, t)
                variance(t, 2 * NT)
                dve.wait_ge(sd_done, 2 * NT + t + 1)
                dve.reciprocal(stat[:, 3, t:t + 1], stat[:, 2, t:t + 1])
                dve.drain()
                dve.scalar_tensor_tensor(out=h[:, t, :], in0=h[:, t, :], scalar=stat[:, 3, t:t + 1], in1=wfin[:],
                                         op0=ALU.mult, op1=ALU.mult).then_inc(out_rdy, 1)

        @blk.tensor
        def _(pe):
            def transposes(src, bank, t, base):
                pe.wait_ge(xn_done, base + t + 1)
                for k in range(KD):
                    ins = pe.transpose(ps[:, bank + k // 4, (k % 4) * P:(k % 4 + 1) * P],
                                       src[:, t % 2, k * P:(k + 1) * P], ident[:])
                ins.then_inc(tr_done, 1)

            pe.wait_ge(vec_ld, 32)
            def first_transposes(t):
                if t >= 2:
                    pe.wait_ge(y_done, t - 1)
                transposes(xn, 4 + 2 * (t % 2), t, 0)

            for t in range(4):
                first_transposes(t)

            def passes(out, w_slot, w0, w1, m, mt, cols, start, stop, stationary_w=True):
                for i, (a, b) in enumerate(((0, 0), (0, 1), (1, 0))):
                    w = split[:, w_slot, a, w0:w1]
                    x = m[:, b, mt, cols[0]:cols[1]]
                    ins = pe.matmul(out, w if stationary_w else x, x if stationary_w else w,
                                    start=start and i == 0, stop=stop and i == 2)
                return ins

            def part(n, slot, bank, i):
                if i == 0:
                    pe.wait_ge(lo_split, n + 1)
                (c0, w), ks = (GROUPS[0], range(2 * i, 2 * i + 2)) if i < 4 else (GROUPS[1], range(4 * (i - 4), 4 * (i - 4) + 4))
                for k in ks:
                    ins = passes(ps[:, bank + (i >= 4), 0:w], slot, k * P, (k + 1) * P, hn, k, (c0, c0 + w), k == 0, k == KD - 1)
                if i == 5:
                    ins.then_inc(unit_done, 1)

            def banks(j):
                return 4 + 2 * (j % 2)

            def score(pr, i):
                a, m = divmod(i, 6)
                c0, w = GROUPS[m // 4]
                if i >= 2:
                    pe.wait_ge(rp, 12 * pr + i - 1)
                own = slice(64 * a, 64 * a + 64)
                pe.matmul(ps[:, 4 + i % 2, 0:w], kdup[:, a, m * P:(m + 1) * P], qsplit[:, a, c0:c0 + w],
                          start=True, stop=False)
                pe.matmul(ps[:, 4 + i % 2, 0:w], klow[own, m * P:(m + 1) * P], qsplit[own, a, c0:c0 + w],
                          start=False, stop=True).then_inc(rs, 1)

            def values(pr, i):
                a, m = divmod(i, 6)
                c0, w = GROUPS[m // 4]
                pe.wait_ge(rp, 12 * pr + i + 1)
                for c in range(w // P):
                    col = c * P + 64 * a
                    ins = pe.matmul(ps[:, 6 + m // 4, col:col + 64], pt[:, (i % 4) * NS + c * P:(i % 4) * NS + (c + 1) * P],
                                    rv[:, m * P + 64 * a:m * P + 64 * a + 64], start=a == 0 and m in (0, 4) and c == 0,
                                    stop=m in (3, 5), skip_group_check=True)
                ins.then_inc(rpv, 1)

            def retention_start(pr):
                pe.wait_ge(kq_lo, pr + 1)
                pe.wait_ge(mv, moved_to(pr, "rvT"))
                score(pr, 0)
                score(pr, 1)

            def retention_part(pr, i):
                values(pr, i)
                if i + 2 < 12:
                    score(pr, i + 2)

            def job(hd, what, first=False):
                j = JOBS.index(what)
                b = banks(j)
                if j == 0:
                    pe.wait_ge(rp, 12 * hd)
                elif j == 1:
                    pe.wait_ge(ro, hd)
                elif first and j < 4:
                    pe.wait_ge(y_done, NT)
                elif JOBS[j - 2] in MERGED:
                    pe.wait_ge(mg, merged_to(hd, JOBS[j - 2]))
                else:
                    pe.wait_ge(mv, moved_to(hd, JOBS[j - 2]))
                out = lambda c0, w: psf[:, b * 512 + c0:b * 512 + c0 + w]
                tok = lambda c: (c * P, (c + 1) * P)
                if what == "diag":
                    pe.wait_ge(qk_done, hd + 1)
                    for c in range(NT):
                        ins = pe.matmul(out(c * P, P), yc[:, c * P:(c + 1) * P], qh[:, c * P:(c + 1) * P], start=True, stop=True)
                elif what in ("hoT", "roT"):
                    x = ("hoT", "roT").index(what)
                    pe.wait_ge(normed, 2 * hd - 1 + x)
                    for c in range(NT):
                        ins = pe.transpose(out(c * P, P), otok[:, x, c * P:(c + 1) * P], ident[:])
                elif what in ("hgT", "rvT"):
                    pe.wait_ge(vt_done, 2 * hd + (1 if what == "hgT" else 2))
                    for c in range(NT):
                        ins = pe.transpose(out(c * P, P), vT[:, c * P:(c + 1) * P], ident[:])
                elif what == "hgPV":
                    pe.wait_ge(mg, merged_to(hd, 64))
                    pe.wait_ge(mv, moved_to(hd, 256))
                    for c in range(NT):
                        keys = range(4) if c < 4 else range(4, 6)
                        for m in keys:
                            s0 = m * NS + c * P if m < 4 else 4 * NS + (m - 4) * NP + (c - 4) * P
                            ins = pe.matmul(out(c * P, P), pt[:, s0:s0 + P], hv[:, m * P:(m + 1) * P],
                                            start=m == keys[0], stop=m == keys[-1])
                elif what < 128:
                    i = what.bit_length() - 1
                    pe.wait_ge(yc_done, 7 * hd + i + 1)
                    pe.wait_ge(q_up, 9 * hd + 1 + i)
                    for c in range(NT):
                        ins = pe.matmul(out(c * P, P), yc[:, c * P:(c + 1) * P], facing(tree_q[:], what, c * P, P),
                                        start=True, stop=True)
                else:
                    i = what.bit_length() - 1
                    pe.wait_ge(q_up, 9 * hd + 1 + i)
                    pe.wait_ge(k_up, 9 * hd + 1 + i)
                    cb_ = what // P
                    for m in range(NT if what == 128 else 4):
                        right = (m // cb_) % 2
                        q0 = (m // (2 * cb_)) * 2 * what + (0 if right else what)
                        ins = pe.matmul(out(m * what, what), tree_k[:, right, m * P:(m + 1) * P],
                                        tree_q[:, 1 - right, q0:q0 + what], start=True, stop=True)
                ins.then_inc(mj, 1)

            WHEN = {(3, 5): "diag", (4, 1): 1, (4, 3): 2, (4, 5): 4, (5, 0): "hgT", (5, 2): 8,
                    (5, 4): 16, (6, 0): 32, (6, 2): 64, (6, 5): 128, (7, 1): 256, (7, 3): "hgPV", (7, 5): "rvT"}

            def mixer_part(hd, first, u, i):
                k = 6 * u + i
                if not first and k == 1:
                    retention_start(hd - 1)
                if not first and 2 <= k < 14:
                    retention_part(hd - 1, k - 2)
                if not first and (u, i) == (3, 2):
                    job(hd, "hoT")
                    job(hd, "roT")
                if u > 3 or (u, i) == (3, 5):
                    if (u, i) in WHEN:
                        job(hd, WHEN[u, i], first)

            def first_units():
                for c in range(NT // 2):
                    for u in range(2):
                        if c == 0:
                            pe.wait_ge(lo_split, u + 1)
                        if u == 0:
                            pe.wait_ge(ylo_done, 2 * c + 2)
                        c0 = 2 * c * P
                        bank = 2 * u + c // 2
                        for k in range(KD):
                            ins = passes(ps[:, bank, c0 % NS:c0 % NS + 2 * P], u, k * P, (k + 1) * P, hn, k,
                                         (c0, c0 + 2 * P), k == 0, k == KD - 1)
                        if c == NT // 2 - 1:
                            ins.then_inc(unit_done, 1)
                        if c == 0:
                            first_transposes(4 + u)

            def mixer(hd, first):
                if first:
                    first_units()
                for u in range(2 if first else 0, U_MIX):
                    after(pe, dfree[u % 2], 4 * hd + u // 2)
                    for i in range(6):
                        part(U_MIX * hd + u, u % 4, 2 * (u % 2), i)
                        mixer_part(hd, first, u, i)

            mixer(0, True)
            with pe.Fori(1, HEADS_H) as hd:
                mixer(hd, False)

            for u in range(HEADS_H):
                pe.wait_ge(dfree[u % 2], 16 + u // 2)
                for i in range(6):
                    part(U_HG + u, u, 2 * (u % 2), i)
                    if (u, i) != (3, 5):
                        mixer_part(HEADS_H, False, u, i)

            with pe.Fori(0, 2) as i2:
                for jj in range(4):
                    n = U_UP + 12 * i2 + 3 * jj
                    j = 4 * i2 + jj
                    for u in range(2):
                        pe.wait_ge(dfree[u], 18 + j)
                        for i in range(6):
                            part(n + u, (3 * jj + u) % 4, 2 * u, i)
                    pe.wait_ge(lo_split, n + 3)
                    pe.wait_ge(glo, KD)
                    pe.wait_ge(upf, j + 1)
                    for kind in range(2):
                        for b, (c0, w) in enumerate(GROUPS):
                            for k in range(4 * kind, 4 * kind + 4):
                                ins = passes(ps[:, 4 + 2 * kind + b, 0:w], (3 * jj + 2) % 4, k * P, (k + 1) * P,
                                             gated, k, (c0, c0 + w), k % 4 == 0, k % 4 == 3)
                    ins.then_inc(unit_done, 1)

            def rows(n, k2, m, mt, t, bank, start, stop):
                return passes(ps[:, bank, :], n % 4, 512 * k2, 512 * k2 + 512, m, mt, (t * P, (t + 1) * P),
                              start, stop, stationary_w=False)

            pe.wait_ge(dfree[0], 26)
            pe.wait_ge(dfree[1], 26)
            for k in range(KD):
                n = U_O0 + k // 2
                if k % 2 == 0:
                    pe.wait_ge(lo_split, n + 1)
                pe.wait_ge(mlo, k + 1)
                for t in range(NT):
                    if k == 0 and t == 4:
                        pe.wait_ge(upf, KD + 1)
                    ins = rows(n, k % 2, merged, k, t, t, k == 0, k == KD - 1)
                    if k == KD - 1:
                        ins.then_inc(w_done, 1)
                if k % 2 == 1:
                    pe.drain().then_inc(unit_done, 1)

            def second_transposes(t):
                if t > 0:
                    pe.wait_ge(y_done, NT + t)
                transposes(hxn, 4, t, NT)

            for t in range(NT):
                if t >= 2:
                    pe.wait_ge(h_up, t - 1)
                for k in range(KD):
                    n = U_O1 + k // 2
                    if t == 0 and k % 2 == 0:
                        pe.wait_ge(lo_split, n + 1)
                    ins = rows(n, k % 2, merged, k, t, (6 + t) % 8, k == 0, k == KD - 1)
                    if t == NT - 1 and k % 2 == 1 and k < KD - 1:
                        ins.then_inc(unit_done, 1)
                ins.then_inc(w_done, 1)
                if t == NT - 1:
                    pe.drain().then_inc(unit_done, 1)
                if t == 1:
                    pe.wait_ge(h_up, NT)
                if t > 0:
                    second_transposes(t - 1)

            def ffn_step(u0, f0, i2, last_tile):
                for ff in range(2):
                    n = u0 + 4 * i2 + 2 * ff
                    f = f0 + 2 * i2 + ff
                    pe.wait_ge(u_free, f + 1)
                    if last_tile and ff == 0:
                        pe.wait_ge(ylo_done, NT + 4)
                        for i in range(4):
                            part(n, 2 * ff, 6, i)
                        second_transposes(NT - 1)
                        pe.wait_ge(v_free, f + 1)
                        for i in range(3):
                            part(n + 1, 2 * ff + 1, 0, i)
                        pe.wait_ge(ylo_done, 2 * NT)
                        for i in (4, 5):
                            part(n, 2 * ff, 6, i)
                        for i in (3, 4, 5):
                            part(n + 1, 2 * ff + 1, 0, i)
                        continue
                    for i in range(6):
                        part(n, 2 * ff, 6, i)
                    pe.wait_ge(v_free, f + 1)
                    for i in range(6):
                        part(n + 1, 2 * ff + 1, 0, i)

            def ffn(u0, f0, i0, steps):
                with pe.Fori(i0, steps) as i2:
                    ffn_step(u0, f0, i2, False)

            def down(u0, u1, tiles, f_done, base, by_token):
                mid = (u0 + u1) // 2
                for half in range(2):
                    for n in range(u0 if half == 0 else mid, mid if half == 0 else u1 - by_token):
                        pe.wait_ge(lo_split, n + 1)
                        first = n in (u0, mid)
                        last = n + 1 in (mid, u1)
                        if first and half == 0:
                            pe.wait_ge(u_free, f_done + 1)
                        if first and half == 1:
                            pe.wait_ge(v_free, f_done + 1)
                        for k2 in range(2):
                            k = 2 * (n - (u0, mid)[half]) + k2
                            if half == 0:
                                pe.wait_ge(g_lo, f_done - tiles + k + 1)
                            for t in range(NT):
                                if first and k2 == 0 and half == 1 and t >= 2:
                                    pe.wait_ge(h_up, base + t - 1)
                                ins = rows(n, k2, g, k, t, (2 + t, t)[half], first and k2 == 0, last and k2 == 1)
                                if last and k2 == 1:
                                    ins.then_inc(dn, 1)
                        pe.drain().then_inc(unit_done, 1)
                for t in range(NT if by_token else 0):
                    for n in range(u1 - by_token, u1):
                        if t == 0:
                            pe.wait_ge(lo_split, n + 1)
                        for k2 in range(2):
                            ins = rows(n, k2, g, 2 * (n - mid) + k2, t, t, False, n == u1 - 1 and k2 == 1)
                    ins.then_inc(dn, 1)

            ffn_step(U_FA, 0, 0, True)
            ffn(U_FA, 0, 1, FA // 2)
            down(U_DA, U_FB, FA, FA, 2 * NT, 0)
            pe.wait_ge(h_up, 4 * NT)
            ffn(U_FB, FA, 0, (NF - FA) // 2)
            down(U_DB, UNITS, NF - FA, NF, 4 * NT, 4)


def _tables():
    f32 = np.float32
    half = DK_R // 2
    inv = (f32(10000.0) ** (-np.arange(half, dtype=f32) / f32(half))).astype(f32)
    pos = np.concatenate([np.arange(NS), np.arange(NP)]).astype(f32)
    ang = (pos[:, None] * inv[None, :]).astype(f32).astype(np.float64)
    cos, sin = np.cos(ang).T, np.sin(ang).T
    rot = np.empty((P, 2, T), f32)
    for q in range(4):
        rot[32 * q:32 * q + 32, 0] = cos
        rot[32 * q:32 * q + 32, 1] = -sin if q % 2 == 0 else sin
    gamma = 1.0 - 2.0 ** (-5.0 - np.arange(HEADS_R))
    dist = np.abs(np.arange(STRIP)[None, :] - np.arange(P)[:, None] - 3 * P)
    strip = (DK_R ** -0.5 * gamma[:, None, None] ** dist[None]).astype(f32)
    strips = np.ascontiguousarray(strip.reshape(PAIRS, 2, P, STRIP).transpose(0, 2, 1, 3)).reshape(PAIRS, P, 2 * STRIP)
    i = np.arange(P)
    masks = np.stack([((i[:, None] // s) ^ 1) == (i[None, :] // s) for s in LEVELS[:7]], 1).astype(f32)
    return rot, np.ascontiguousarray(masks), strips


def _units(w_in, w_ret_up, w_hg_up, w_out, w_ffn_in, w_ffn_down):
    def cols(w, c0):
        return w[:, c0:c0 + P].reshape(KD, P, P).transpose(1, 0, 2).reshape(P, UNIT)

    def rows(w, k, half):
        return w[2 * k * P:2 * (k + 1) * P, 512 * half:512 * half + 512].reshape(2, P, 512).transpose(1, 0, 2).reshape(P, UNIT)

    rq, rk, rv, rg, hq, ff, fb, hi, hg, ga, gb = 0, 512, 1024, 1536, 2048, 2560, 3072, 3584, 4096, 4608, 5632
    out = []
    for i in range(HEADS_H):
        out += [cols(w_in, c + i * P) for c in (ff, fb, hq, hi, rq, rk, rv, rg)]
    out += [cols(w_in, hg + i * P) for i in range(HEADS_H)]
    up = np.concatenate([w_ret_up, w_hg_up], 0)
    for j in range(KD):
        out += [cols(w_in, ga + j * P), cols(w_in, gb + j * P), cols(up, j * P)]
    out += [rows(w_out, k, half) for half in range(2) for k in range(KD // 2)]
    for f0, f1 in ((0, FA), (FA, NF)):
        for f in range(f0, f1):
            out += [cols(w_ffn_in, f * P), cols(w_ffn_in, FF + f * P)]
        out += [rows(w_ffn_down, k, half) for half in range(2) for k in range(f0 // 2, f1 // 2)]
    assert len(out) == UNITS
    return np.stack(out)


def kernel(**inputs):
    from concourse import bacc
    from concourse.bass_utils import run_bass_kernel_spmd

    a = {k: np.asarray(v) for k, v in inputs.items()}
    rot, masks, strips = _tables()
    tiles = lambda v: v.reshape(-1, P).T
    vec = np.concatenate(
        [tiles(a["norm_mix"][0]), tiles(a["norm_ffn"][0]), tiles(a["w_ret_norm"][0]), tiles(a["w_hg_norm"][0])]
        + [tiles(a["conv_w"][0, i]) for i in range(3)] + [tiles(a["conv_b"][0])]
        + [tiles(a["lower_bounds"][r, d]) for r in range(2) for d in range(2)], 1)
    arrays = {
        "x_s": a["x_sample"][0], "x_p": a["x_prompt"][0],
        "units": _units(a["w_in"][0], a["w_ret_up"][0], a["w_hg_up"][0], a["w_out"][0], a["w_ffn_in"][0], a["w_ffn_down"][0]),
        "vec": vec, "w_final": np.broadcast_to(a["norm_final"][None, :], (P, D)),
        "ident": np.eye(P, dtype=np.float32), "masks": masks, "rot": rot, "strips": strips,
    }
    arrays = {f"in_{k}": np.ascontiguousarray(v) for k, v in arrays.items()}
    nc = bacc.Bacc("TRN2", target_bir_lowering=False, num_devices=1, dynamic_dma_scratch_size=1024)
    args = [nc.dram_tensor(k, v.shape, mybir.dt.from_np(v.dtype), kind="ExternalInput").ap() for k, v in arrays.items()]
    outs = [nc.dram_tensor(k, [n, D], F32, kind="ExternalOutput").ap() for k, n in (("y_s", NS), ("y_p", NP))]
    build(nc, *args, *outs)
    r = run_bass_kernel_spmd(nc, [arrays], core_ids=[0]).results[0]
    return r["y_p"].reshape(1, NP, D), r["y_s"].reshape(1, NS, D)
```
